# Optimizing a Trainium2 kernel written in Bass

```python
import math, functools
import jax, jax.numpy as jnp
from jax import lax
import numpy as np

D_MODEL = 1024
BATCH = 1
SEQ = 1024
DEPTH = 1
DEC_BATCH = 8
DEC_SEQ = 1
PAST_LEN = 8192
PAGE_SIZE = 128

MIX_WIDTH = D_MODEL
SB_WIDTH = MIX_WIDTH // 2
SSM_WIDTH = MIX_WIDTH - SB_WIDTH
SB_HEAD_DIM = 64
SB_HEADS = SB_WIDTH // SB_HEAD_DIM
SB_BIAS_INIT = -8.0
SSM_GROUP = 16
SSM_GROUPS = SSM_WIDTH // SSM_GROUP
SSM_STATE = 64
D_FF = 2816
N_MEM = 256
X_HEADS = 4
X_HEAD_DIM = D_MODEL // X_HEADS
Q_BLOCK = 128
EPS = 1e-6
DT_MIN = 0.001
DT_MAX = 0.1
A_RE_CLIP = -1e-4

kernel_name = 'hymba_stickbreak_s5_macaron_step'

F32 = jnp.float32

def rmsnorm(x, g):
    xf = x.astype(F32)
    y = xf * lax.rsqrt(jnp.mean(xf * xf, axis=-1, keepdims=True) + EPS)
    return (y * g.astype(F32)).astype(x.dtype)

def half_ffn(x, g, w_gate, w_up, w_down):
    h = rmsnorm(x, g)
    return x + 0.5 * ((jax.nn.silu(h @ w_gate) * (h @ w_up)) @ w_down)

def sb_weights(z, q_pos, k_pos):
    mask = k_pos[None, :] < q_pos[:, None]
    log_keep = jnp.where(mask, jax.nn.log_sigmoid(-z), 0.0)
    after = lax.cumsum(log_keep, axis=z.ndim - 1, reverse=True) - log_keep
    return jnp.where(mask, jnp.exp(jax.nn.log_sigmoid(z) + after), 0.0)

def sb_prompt(q, k, v, bias):
    b, l, h, d = q.shape
    nb = l // Q_BLOCK
    scale = d ** -0.5
    k_pos = jnp.arange(l)
    bias_f = bias.astype(F32)[None, :, None, None]
    qb = q.reshape(b, nb, Q_BLOCK, h, d).transpose(1, 0, 2, 3, 4)
    qpos = jnp.arange(l).reshape(nb, Q_BLOCK)

    def block(args):
        q_blk, q_p = args
        z = jnp.einsum('bqhd,bkhd->bhqk', q_blk, k).astype(F32) * scale + bias_f
        w = sb_weights(z, q_p, k_pos)
        return jnp.einsum('bhqk,bkhd->bqhd', w.astype(v.dtype), v)

    o = lax.map(block, (qb, qpos))
    return o.transpose(1, 0, 2, 3, 4).reshape(b, l, h * d)

def sb_sample(q, k_new, v_new, bias, k_past, v_past):
    b, l, h, d = q.shape
    past = k_past.shape[1]
    scale = d ** -0.5
    q_pos = past + jnp.arange(l)
    k_pos = jnp.arange(past + l)
    bias_f = bias.astype(F32)[None, :, None, None]
    z = jnp.concatenate([jnp.einsum('bqhd,bkhd->bhqk', q, k_past),
                         jnp.einsum('bqhd,bkhd->bhqk', q, k_new)], axis=-1).astype(F32) * scale + bias_f
    w = sb_weights(z, q_pos, k_pos).astype(v_new.dtype)
    o = (jnp.einsum('bhqk,bkhd->bqhd', w[..., :past], v_past)
         + jnp.einsum('bhqk,bkhd->bqhd', w[..., past:], v_new))
    return o.reshape(b, l, h * d)

def s5_discretize(a_re, a_im, log_dt, b_re, b_im):
    dt = jnp.exp(log_dt.astype(F32))[:, None]
    lam_re = jnp.minimum(a_re.astype(F32), A_RE_CLIP)
    lam_im = a_im.astype(F32)
    mag = jnp.exp(lam_re * dt)
    ab_re = mag * jnp.cos(lam_im * dt)
    ab_im = mag * jnp.sin(lam_im * dt)
    den = lam_re * lam_re + lam_im * lam_im
    nr = ab_re - 1.0
    f_re = (nr * lam_re + ab_im * lam_im) / den
    f_im = (ab_im * lam_re - nr * lam_im) / den
    br = b_re.astype(F32)
    bi = b_im.astype(F32)
    bb_re = f_re[..., None] * br - f_im[..., None] * bi
    bb_im = f_re[..., None] * bi + f_im[..., None] * br
    return ab_re, ab_im, bb_re, bb_im

def _complex_affine_combine(e1, e2):
    a1r, a1i, b1r, b1i = e1
    a2r, a2i, b2r, b2i = e2
    return (a2r * a1r - a2i * a1i, a2r * a1i + a2i * a1r,
            a2r * b1r - a2i * b1i + b2r, a2r * b1i + a2i * b1r + b2i)

def s5_mix(u, s0_re, s0_im, a_re, a_im, log_dt, b_re, b_im, c_re, c_im, d_skip, w_glu, b_glu):
    bsz, l, _ = u.shape
    uf = u.astype(F32)
    ug = uf.reshape(bsz, l, SSM_GROUPS, SSM_GROUP)
    ab_re, ab_im, bb_re, bb_im = s5_discretize(a_re, a_im, log_dt, b_re, b_im)
    bu_re = jnp.einsum('blgc,gpc->blgp', ug, bb_re)
    bu_im = jnp.einsum('blgc,gpc->blgp', ug, bb_im)
    a_r = jnp.broadcast_to(ab_re, bu_re.shape)
    a_i = jnp.broadcast_to(ab_im, bu_im.shape)
    p_re, p_im, s_re, s_im = lax.associative_scan(
        _complex_affine_combine, (a_r, a_i, bu_re, bu_im), axis=1)
    if s0_re is not None:
        s0r = s0_re.astype(F32)[:, None]
        s0i = s0_im.astype(F32)[:, None]
        s_re, s_im = (s_re + p_re * s0r - p_im * s0i,
                      s_im + p_re * s0i + p_im * s0r)
    y = (jnp.einsum('blgp,gcp->blgc', s_re, c_re.astype(F32))
         - jnp.einsum('blgp,gcp->blgc', s_im, c_im.astype(F32)))
    y = y.reshape(bsz, l, SSM_WIDTH) + d_skip.astype(F32) * uf
    g = jax.nn.gelu(y)
    out = g * jax.nn.sigmoid(g @ w_glu.astype(F32) + b_glu.astype(F32))
    return out.astype(u.dtype), s_re[:, -1], s_im[:, -1]

def memory_kv(mem, g_mem, w_xk, w_xv):
    b, m, _ = mem.shape
    hm = rmsnorm(mem, g_mem)
    return ((hm @ w_xk).reshape(b, m, X_HEADS, X_HEAD_DIM),
            (hm @ w_xv).reshape(b, m, X_HEADS, X_HEAD_DIM))

def cross_attend(h, w_xq, w_xo, mem_k, mem_v):
    b, l, _ = h.shape
    q = (h @ w_xq).reshape(b, l, X_HEADS, X_HEAD_DIM)
    s = jnp.einsum('blhd,bmhd->bhlm', q, mem_k).astype(F32) * (X_HEAD_DIM ** -0.5)
    p = jax.nn.softmax(s, axis=-1).astype(mem_v.dtype)
    o = jnp.einsum('bhlm,bmhd->blhd', p, mem_v).reshape(b, l, D_MODEL)
    return o @ w_xo

def layer_step(x, lp, sb_fn, s0_re, s0_im, mem_k, mem_v):
    b, l, _ = x.shape
    x = half_ffn(x, lp['g_ffn1'], lp['w_ffn1_gate'], lp['w_ffn1_up'], lp['w_ffn1_down'])
    h = rmsnorm(x, lp['g_mix'])
    proj = h @ lp['w_in']
    q, k, v, u = jnp.split(proj, [SB_WIDTH, 2 * SB_WIDTH, 3 * SB_WIDTH], axis=-1)
    q = q.reshape(b, l, SB_HEADS, SB_HEAD_DIM)
    k = k.reshape(b, l, SB_HEADS, SB_HEAD_DIM)
    v = v.reshape(b, l, SB_HEADS, SB_HEAD_DIM)
    o_sb = sb_fn(q, k, v, lp['sb_bias'])
    o_ssm, s_re, s_im = s5_mix(u, s0_re, s0_im, lp['ssm_a_re'], lp['ssm_a_im'], lp['ssm_log_dt'],
                               lp['ssm_b_re'], lp['ssm_b_im'], lp['ssm_c_re'], lp['ssm_c_im'],
                               lp['ssm_d'], lp['w_glu'], lp['b_glu'])
    mixed = jnp.concatenate([rmsnorm(o_sb, lp['g_sb_out']), rmsnorm(o_ssm, lp['g_ssm_out'])], axis=-1)
    x = x + mixed @ lp['w_out']
    x = x + cross_attend(rmsnorm(x, lp['g_xattn']), lp['w_xq'], lp['w_xo'], mem_k, mem_v)
    x = half_ffn(x, lp['g_ffn2'], lp['w_ffn2_gate'], lp['w_ffn2_up'], lp['w_ffn2_down'])
    return x, k, v, s_re, s_im

def setup_inputs(seed: int = 0) -> dict:
    key = jax.random.key(seed)
    ks = iter(jax.random.split(key, 48))

    def nrm(shape, scale):
        return jax.random.normal(next(ks), shape, F32) * scale

    def gain(shape):
        return 1.0 + 0.02 * jax.random.normal(next(ks), shape, F32)

    L = DEPTH
    n_pages = PAST_LEN // PAGE_SIZE
    n_used = DEC_BATCH * n_pages
    n_pool = n_used + max(1, n_used // 4)
    dm = D_MODEL ** -0.5
    inp = {}
    inp['x_prompt'] = nrm((BATCH, SEQ, D_MODEL), 1.0)
    inp['x_sample'] = nrm((DEC_BATCH, DEC_SEQ, D_MODEL), 1.0)
    inp['cache_k'] = nrm((L, n_pool, PAGE_SIZE, SB_HEADS, SB_HEAD_DIM), 1.0)
    inp['cache_v'] = nrm((L, n_pool, PAGE_SIZE, SB_HEADS, SB_HEAD_DIM), 1.0)
    inp['state_ssm_re'] = nrm((L, DEC_BATCH, SSM_GROUPS, SSM_STATE), 0.5)
    inp['state_ssm_im'] = nrm((L, DEC_BATCH, SSM_GROUPS, SSM_STATE), 0.5)
    inp['cache_mem_k'] = nrm((L, DEC_BATCH, N_MEM, X_HEADS, X_HEAD_DIM), 1.0)
    inp['cache_mem_v'] = nrm((L, DEC_BATCH, N_MEM, X_HEADS, X_HEAD_DIM), 1.0)
    inp['page_table'] = jax.random.permutation(next(ks), n_pool)[:n_used].reshape(
        DEC_BATCH, n_pages).astype(jnp.int32)
    inp['mem_prompt'] = nrm((BATCH, N_MEM, D_MODEL), 1.0)
    inp['g_ffn1'] = gain((L, D_MODEL))
    inp['w_ffn1_gate'] = nrm((L, D_MODEL, D_FF), dm)
    inp['w_ffn1_up'] = nrm((L, D_MODEL, D_FF), dm)
    inp['w_ffn1_down'] = nrm((L, D_FF, D_MODEL), D_FF ** -0.5)
    inp['g_mix'] = gain((L, D_MODEL))
    inp['w_in'] = nrm((L, D_MODEL, 3 * SB_WIDTH + SSM_WIDTH), dm)
    inp['sb_bias'] = SB_BIAS_INIT + nrm((L, SB_HEADS), 0.1)
    inp['ssm_a_re'] = -0.5 + nrm((L, SSM_GROUPS, SSM_STATE), 0.01)
    inp['ssm_a_im'] = (jnp.pi * jnp.arange(SSM_STATE, dtype=F32))[None, None, :] + nrm(
        (L, SSM_GROUPS, SSM_STATE), 0.01)
    inp['ssm_log_dt'] = jax.random.uniform(next(ks), (L, SSM_GROUPS), F32,
                                           math.log(DT_MIN), math.log(DT_MAX))
    inp['ssm_b_re'] = nrm((L, SSM_GROUPS, SSM_STATE, SSM_GROUP), (2 * SSM_GROUP) ** -0.5)
    inp['ssm_b_im'] = nrm((L, SSM_GROUPS, SSM_STATE, SSM_GROUP), (2 * SSM_GROUP) ** -0.5)
    inp['ssm_c_re'] = nrm((L, SSM_GROUPS, SSM_GROUP, SSM_STATE), (2 * SSM_STATE) ** -0.5)
    inp['ssm_c_im'] = nrm((L, SSM_GROUPS, SSM_GROUP, SSM_STATE), (2 * SSM_STATE) ** -0.5)
    inp['ssm_d'] = nrm((L, SSM_WIDTH), 1.0)
    inp['w_glu'] = nrm((L, SSM_WIDTH, SSM_WIDTH), SSM_WIDTH ** -0.5)
    inp['b_glu'] = nrm((L, SSM_WIDTH), 0.01)
    inp['g_sb_out'] = gain((L, SB_WIDTH))
    inp['g_ssm_out'] = gain((L, SSM_WIDTH))
    inp['w_out'] = nrm((L, MIX_WIDTH, D_MODEL), MIX_WIDTH ** -0.5)
    inp['g_xattn'] = gain((L, D_MODEL))
    inp['g_mem'] = gain((L, D_MODEL))
    inp['w_xq'] = nrm((L, D_MODEL, D_MODEL), dm)
    inp['w_xk'] = nrm((L, D_MODEL, D_MODEL), dm)
    inp['w_xv'] = nrm((L, D_MODEL, D_MODEL), dm)
    inp['w_xo'] = nrm((L, D_MODEL, D_MODEL), dm)
    inp['g_ffn2'] = gain((L, D_MODEL))
    inp['w_ffn2_gate'] = nrm((L, D_MODEL, D_FF), dm)
    inp['w_ffn2_up'] = nrm((L, D_MODEL, D_FF), dm)
    inp['w_ffn2_down'] = nrm((L, D_FF, D_MODEL), D_FF ** -0.5)
    inp['g_final'] = gain((D_MODEL,))
    return inp

def reference(x_prompt, x_sample, cache_k, cache_v, state_ssm_re, state_ssm_im,
              cache_mem_k, cache_mem_v, page_table, mem_prompt,
              g_ffn1, w_ffn1_gate, w_ffn1_up, w_ffn1_down, g_mix, w_in, sb_bias,
              ssm_a_re, ssm_a_im, ssm_log_dt, ssm_b_re, ssm_b_im, ssm_c_re, ssm_c_im,
              ssm_d, w_glu, b_glu, g_sb_out, g_ssm_out, w_out,
              g_xattn, g_mem, w_xq, w_xk, w_xv, w_xo,
              g_ffn2, w_ffn2_gate, w_ffn2_up, w_ffn2_down, g_final):
    dec_b = page_table.shape[0]
    yp, ys = x_prompt, x_sample
    kp_l, vp_l, ks_l, vs_l = [], [], [], []
    srp_l, sip_l, srs_l, sis_l = [], [], [], []
    mkp_l, mvp_l = [], []
    for l in range(DEPTH):
        lp = dict(g_ffn1=g_ffn1[l], w_ffn1_gate=w_ffn1_gate[l], w_ffn1_up=w_ffn1_up[l],
                  w_ffn1_down=w_ffn1_down[l], g_mix=g_mix[l], w_in=w_in[l], sb_bias=sb_bias[l],
                  ssm_a_re=ssm_a_re[l], ssm_a_im=ssm_a_im[l], ssm_log_dt=ssm_log_dt[l],
                  ssm_b_re=ssm_b_re[l], ssm_b_im=ssm_b_im[l], ssm_c_re=ssm_c_re[l],
                  ssm_c_im=ssm_c_im[l], ssm_d=ssm_d[l], w_glu=w_glu[l], b_glu=b_glu[l],
                  g_sb_out=g_sb_out[l], g_ssm_out=g_ssm_out[l], w_out=w_out[l],
                  g_xattn=g_xattn[l], w_xq=w_xq[l], w_xo=w_xo[l],
                  g_ffn2=g_ffn2[l], w_ffn2_gate=w_ffn2_gate[l], w_ffn2_up=w_ffn2_up[l],
                  w_ffn2_down=w_ffn2_down[l])
        mk_p, mv_p = memory_kv(mem_prompt, g_mem[l], w_xk[l], w_xv[l])
        yp, kp, vp, srp, sip = layer_step(yp, lp, sb_prompt, None, None, mk_p, mv_p)
        k_past = cache_k[l][page_table].reshape(dec_b, -1, SB_HEADS, SB_HEAD_DIM)
        v_past = cache_v[l][page_table].reshape(dec_b, -1, SB_HEADS, SB_HEAD_DIM)
        sb_fn = functools.partial(sb_sample, k_past=k_past, v_past=v_past)
        ys, ksm, vsm, srs, sis = layer_step(ys, lp, sb_fn, state_ssm_re[l], state_ssm_im[l],
                                            cache_mem_k[l], cache_mem_v[l])
        kp_l.append(kp); vp_l.append(vp); ks_l.append(ksm); vs_l.append(vsm)
        srp_l.append(srp); sip_l.append(sip); srs_l.append(srs); sis_l.append(sis)
        mkp_l.append(mk_p); mvp_l.append(mv_p)
    y_prompt = rmsnorm(yp, g_final)
    y_sample = rmsnorm(ys, g_final)
    return (y_prompt, y_sample,
            jnp.stack(kp_l), jnp.stack(vp_l), jnp.stack(ks_l), jnp.stack(vs_l),
            jnp.stack(srp_l), jnp.stack(sip_l), jnp.stack(srs_l), jnp.stack(sis_l),
            jnp.stack(mkp_l), jnp.stack(mvp_l))


_drawn_inputs = setup_inputs


def setup_inputs(seed=0):
    import zlib

    import numpy as np

    out = dict(_drawn_inputs(seed))
    spreads = {}
    factors = {'g_ffn1': 5.635,
     'g_mix': 2.701,
     'ssm_a_re': 58.089,
     'b_glu': 37.161,
     'g_sb_out': 96.24,
     'g_ssm_out': 84.588,
     'g_xattn': 44.762,
     'g_mem': 8.319,
     'g_ffn2': 24.536}
    for name, (base, spread) in spreads.items():
        noise = np.random.default_rng([zlib.crc32(name.encode()), seed]).standard_normal(out[name].shape)
        drawn = base * np.exp(spread * noise) if base else spread * noise
        out[name] = __import__('jax').numpy.asarray(drawn.astype(out[name].dtype))
    for name, factor in factors.items():
        out[name] = (out[name] * factor).astype(out[name].dtype)
    return out
```

```python
import math
from contextlib import ExitStack

import concourse.bass as bass
from concourse import mybir
from concourse.alu_op_type import AluOpType as ALU

F32 = mybir.dt.float32
F32R = mybir.dt.float32r
I32 = mybir.dt.int32
ACT = mybir.ActivationFunctionType
AX = mybir.AxisListType
ds = bass.ds

P = 128
EPS = 1e-6
KD = 8
NP = 1024
NS = 8
NT = NP + NS
D = 1024
FF = 2816
RAW_RING = 2
W_RING = 3
PROMPT_TILES = [(0, 512), (512, 512)]
ALL_TILES = [(0, 344), (344, 344), (688, 344)]
PI2_MID = 0.0019350051879882812
PI2_LOW = 2 * math.pi - 6.28125 - PI2_MID
PI_BELOW = 3.1415925


class Stream:

    def __init__(self, k, name, width=D):
        self.k, self.width = k, width
        self.landed = [k.sem(f"{name}_landed{r}") for r in range(RAW_RING)]
        self.hi_done = k.sem(f"{name}_hi_done")
        self.lo_done = k.sem(f"{name}_lo_done")

    def credits_dve(self, dve):
        dve.sem_inc(self.lo_done, RAW_RING)

    def load(self, eng, n, c, src, shape=None):
        eng.wait_ge(self.lo_done, n + 1)
        dst = self.k.raw[:, c % RAW_RING, 0:self.width]
        if shape:
            dst = dst.rearrange("p (k m) -> p k m", k=shape)
        eng.dma_start(dst, src).then_inc(self.landed[c % RAW_RING], 16)

    def hi(self, act, n, c, turn, free=None, used=None):
        act.wait_ge(self.landed[c % RAW_RING], turn * 16)
        if free is not None:
            act.wait_ge(free, used)
        act.activation(self.k.whi[c % W_RING][:, 0:self.width], self.k.raw[:, c % RAW_RING, 0:self.width], ACT.Copy).then_inc(self.hi_done, 1)

    def lo(self, dve, n, c):
        dve.wait_ge(self.hi_done, n + 1)
        dve.tensor_tensor(self.k.wlo[c % W_RING][:, 0:self.width], self.k.raw[:, c % RAW_RING, 0:self.width],
                          self.k.whi[c % W_RING][:, 0:self.width].bitcast(F32), ALU.subtract).then_inc(self.lo_done, 1)

    def ready(self, pe, n):
        pe.wait_ge(self.lo_done, n + 1 + RAW_RING)


def each_unit(eng, count, body):
    full = count // 6
    if full > 1:
        with eng.Fori(0, full) as i:
            for c in range(6):
                body(i * 6 + c, c, i * 3 + (c // 2 + 1))
    elif full:
        for c in range(6):
            body(c, c, c // 2 + 1)
    for n in range(full * 6, count):
        body(n, n % 6, n // 2 + 1)


def three_passes(pe, out, whi, wlo, rhi, rlo, first, last):
    pe.matmul(out, whi, rhi, start=first, stop=False)
    pe.matmul(out, whi, rlo, start=False, stop=False)
    return pe.matmul(out, wlo, rhi, start=False, stop=last)

class Norm:

    def __init__(self, k, name, tiles, src, blocks, gain, hi, lo, square, tmp, root, aux, banks, first=None):
        self.first = first or (lambda t: 0)
        self.k, self.tiles, self.src, self.blocks, self.gain = k, tiles, src, blocks, gain
        self.hi, self.lo, self.square, self.tmp, self.root, self.aux, self.banks = hi, lo, square, tmp, root, aux, banks
        self.squared, self.summed, self.rooted, self.inverse, self.scaled, self.hi_done, self.lo_done = (
            k.sem(f"{name}_{s}") for s in ("squared", "summed", "rooted", "inverse", "scaled", "hi_done", "lo_done"))

    def act(self, act):
        B = self.blocks

        def squares(t, k):
            t0, n = self.tiles[t]
            if t * B + k >= 2:
                act.wait_ge(self.summed, t * B + k - 1)
            act.activation(self.square[:, (t * B + k) % 2, 0:n], self.src(self.first(t) + k, t0, n), ACT.Square).then_inc(self.squared, 1)

        def hi(t, k):
            t0, n = self.tiles[t]
            act.wait_ge(self.scaled, t * B + k + 1)
            act.activation(self.hi[:, self.first(t) + k, t0:t0 + n], self.tmp[:, (t * B + k) % 2, 0:n], ACT.Copy).then_inc(self.hi_done, 1)

        for t in range(len(self.tiles) + 1):
            if t < len(self.tiles):
                n = self.tiles[t][1]
                for k in range(B):
                    squares(t, k)
                    if t and self.lo is not None:
                        hi(t - 1, k)
                act.wait_ge(self.summed, (t + 1) * B)
                if t:
                    act.wait_ge(self.inverse, 6 * t)
                act.activation(self.aux[:, 0, 0:n], self.k.ps[self.banks[t]][:, 0:n], ACT.Copy, scale=1.0 / (B * P),
                               bias=EPS).then_inc(self.rooted, 1)
                act.wait_ge(self.rooted, 2 * t + 1)
                act.activation(self.root[:, t % 3, 0:n], self.aux[:, 0, 0:n], ACT.Sqrt).then_inc(self.rooted, 1)
            elif self.lo is not None:
                for k in range(B):
                    hi(t - 1, k)

    def pe(self, pe):
        B = self.blocks
        for t, (t0, n) in enumerate(self.tiles):
            for k in range(B):
                pe.wait_ge(self.squared, t * B + k + 1)
                pe.matmul(self.k.ps[self.banks[t]][:, 0:n], self.k.ones[:, :], self.square[:, (t * B + k) % 2, 0:n],
                          start=k == 0, stop=k == B - 1).then_inc(self.summed, 1)

    def dve(self, v):
        B = self.blocks
        total = len(self.tiles) * B

        def lo(m):
            t0, n = self.tiles[m // B]
            v.wait_ge(self.hi_done, m + 1)
            b = self.first(m // B) + m % B
            v.tensor_tensor(self.lo[:, b, t0:t0 + n], self.tmp[:, m % 2, 0:n],
                            self.hi[:, b, t0:t0 + n].bitcast(F32), ALU.subtract).then_inc(self.lo_done, 1)

        for m in range(total):
            t, k = divmod(m, B)
            t0, n = self.tiles[t]
            if k == 0:
                v.wait_ge(self.rooted, 2 * t + 2)
                r, mean, t_ = self.root[:, t % 3, 0:n], self.aux[:, 0, 0:n], self.aux[:, 1, 0:n]
                for j, step in enumerate((
                        lambda: v.reciprocal(r, r),
                        lambda: v.tensor_tensor(t_, r, r, ALU.mult),
                        lambda: v.tensor_tensor(t_, t_, mean, ALU.mult),
                        lambda: v.tensor_scalar(t_, t_, -0.5, 1.5, ALU.mult, ALU.add),
                        lambda: v.tensor_tensor(r, r, t_, ALU.mult))):
                    step().then_inc(self.inverse, 2 if j == 4 else 1)
                    v.wait_ge(self.inverse, 6 * t + j + (2 if j == 4 else 1))
            split, b = self.lo is not None, self.first(t) + k
            if m >= 2 and split:
                v.wait_ge(self.lo_done, m - 1)
            v.scalar_tensor_tensor(out=self.tmp[:, m % 2, 0:n] if split else self.hi[:, b, t0:t0 + n],
                                   in0=self.src(b, t0, n), scalar=self.gain(b),
                                   in1=self.root[:, t % 3, 0:n], op0=ALU.mult, op1=ALU.mult).then_inc(self.scaled, 1)
            if m and split:
                lo(m - 1)
        if self.lo is not None:
            lo(total - 1)

    def ready(self, pe):
        pe.wait_ge(self.lo_done if self.lo is not None else self.scaled, len(self.tiles) * self.blocks)


class Project:

    def __init__(self, k, name, count, src, hi, lo, tiles, banks, blocks=KD):
        self.k, self.count, self.src, self.hi_, self.lo_ = k, count, src, hi, lo
        self.tiles, self.banks, self.blocks = tiles, banks, blocks
        self.w = Stream(k, name, blocks * P)
        self.summed = k.sem(f"{name}_summed")
        self.drained = k.sem(f"{name}_drained")
        assert 6 * len(tiles) % len(banks) == 0 and (count < 12 or count % 6 >= 3)

    def bank(self, c, t):
        return self.banks[(c * len(self.tiles) + t) % len(self.banks)]

    def sp(self, sp):
        each_unit(sp, self.count, lambda n, c, turn: self.w.load(sp, n, c, self.src(n, c, turn - 1), self.blocks))

    def credits_dve(self, v):
        self.w.credits_dve(v)

    def credits_drain(self, eng):
        eng.sem_inc(self.drained, len(self.banks))

    def act(self, act, drain=None, ahead=True):
        T = len(self.tiles)

        def hi(n, c, turn):
            self.w.hi(act, n, c, turn, self.summed, n * T + T)

        def step(n, c, turn):
            self.half = turn - 1
            if drain:
                for t, (t0, size) in enumerate(self.tiles):
                    act.wait_ge(self.summed, n * T + (t + 1 + W_RING * T))
                    drain(n, c, t, t0, size, self.bank(c, t))
            if not isinstance(n, int) or n + 3 < self.count:
                hi(n + 3, (c + 3) % 6, turn + ((c + 3) // 2 - c // 2))
        if ahead:
            self.act_ahead(act)
        each_unit(act, self.count, step)

    def act_ahead(self, act):
        for n in range(3):
            self.w.hi(act, n, n, n // 2 + 1)

    def dve_ahead(self, v):
        for n in range(3):
            self.w.lo(v, n, n)

    def dve(self, v, drain=None, ahead=True):
        T = len(self.tiles)

        def step(n, c, turn):
            if drain:
                for t, (t0, size) in enumerate(self.tiles):
                    v.wait_ge(self.summed, n * T + (t + 1 + W_RING * T))
                    drain(n, c, t, t0, size, self.bank(c, t))
            if not isinstance(n, int) or n + 3 < self.count:
                self.w.lo(v, n + 3, (c + 3) % 6)
        if ahead:
            self.dve_ahead(v)
        each_unit(v, self.count, step)

    def pe(self, pe):
        T = len(self.tiles)
        pe.sem_inc(self.summed, W_RING * T)

        def step(n, c, turn):
            self.w.ready(pe, n)
            for t, (t0, size) in enumerate(self.tiles):
                pe.wait_ge(self.drained, n * T + (t + 1))
                for k in range(self.blocks):
                    i = three_passes(pe, self.k.ps[self.bank(c, t)][:, 0:size],
                                     self.k.whi[c % 3][:, k * P:(k + 1) * P], self.k.wlo[c % 3][:, k * P:(k + 1) * P],
                                     self.hi_[:, k, t0:t0 + size], self.lo_[:, k, t0:t0 + size], k == 0,
                                     k == self.blocks - 1)
                i.then_inc(self.summed, 1)
        each_unit(pe, self.count, step)


class Decode:

    PAGES = 64
    KC = 2
    KR = 4
    VR = 8

    def __init__(self, k, name):
        self.k, a = k, k.a
        self.keys = a["cache_k"].rearrange("g p n -> p g n")
        self.values = a["cache_v"].rearrange("g p n -> p g n")
        self.kt = k.at(f"{name}_kt", [P, self.KR, self.KC * 512])
        self.vt = k.at(f"{name}_vt", [P, self.VR, 512])
        self.q = k.at(f"{name}_q", [P, 512])
        self.z = k.at(f"{name}_z", [P, 512])
        self.zb = k.at(f"{name}_zb", [P, 512])
        self.e = k.at(f"{name}_e", [P, 512])
        self.w = k.at(f"{name}_w", [P, 512])
        self.mask = k.at(f"{name}_mask", [NS, 512])
        self.own = k.at(f"{name}_own", [NS, 512])
        self.tri = k.at(f"{name}_tri", [P, P])
        self.bias = k.at(f"{name}_bias", [P, NS])
        self.pages = k.at(f"{name}_pages", [1, NS * self.PAGES], I32)
        self.tables_in = k.sem(f"{name}_tables_in")
        self.consts = k.sem(f"{name}_consts")
        self.q_in = k.sem(f"{name}_q_in")
        self.k_in = [k.sem(f"{name}_k_in{r}") for r in range(self.KR)]
        self.v_in = [k.sem(f"{name}_v_in{r}") for r in range(self.VR)]
        self.k_times_q = k.sem(f"{name}_k_times_q")
        self.scored = k.sem(f"{name}_scored")
        self.biased = k.sem(f"{name}_biased")
        self.kept = k.sem(f"{name}_kept")
        self.softplus_done = k.sem(f"{name}_softplus")
        self.sums = k.sem(f"{name}_sums")
        self.later = k.sem(f"{name}_later")
        self.logw = k.sem(f"{name}_logw")
        self.weighted = k.sem(f"{name}_w_done")
        self.v_used = k.sem(f"{name}_v_used")
        self.own_done = k.sem(f"{name}_own_done")
        self.columns_done = k.sem(f"{name}_columns")
        self.stored = k.sem(f"{name}_stored")

    def load_tables(self, sp):
        sp.dma_start(self.pages[:, :], self.k.a["page_table"].rearrange("b g -> (b g)").rearrange("(a n) -> a n", a=1)).then_inc(self.tables_in, 16)
        sp.dma_start(self.bias[:, :], self.k.a["sb_bias"].rearrange("(a n) -> a n", a=1).to_broadcast([P, NS])).then_inc(self.tables_in, 16)
        sp.wait_ge(self.tables_in, 32)

    def load_k(self, sp, b, c):
        if c == 0:
            sp.wait_ge(self.scored, b * 32 + self.KR)
            sp.dma_start(self.q[:, :], self.k.qs_dram[ds(b, 1), :].to_broadcast([P, 512])).then_inc(self.q_in, 16)
        sp.wait_ge(self.scored, b * 32 + (c + 1))
        for j in range(self.KC):
            page = sp.value_load(self.pages[0:1, ds(b * self.PAGES + (c * self.KC + j), 1)], min_val=0, max_val=639)
            sp.dma_start(self.kt[:, c % self.KR, j * 512:(j + 1) * 512], self.keys[:, ds(page, 1), :]).then_inc(self.k_in[c % self.KR], 16)

    def prepare(self, pool):
        pool.sem_inc(self.v_used, self.VR)
        pool.memset(self.tri[:, :], 1.0).then_inc(self.consts, 1)
        pool.memset(self.mask[:, :], 1.0).then_inc(self.consts, 1)
        pool.wait_ge(self.consts, 2)
        pool.affine_select(out=self.tri[:, :], in_=self.tri[:, :], compare_op=ALU.is_ge, fill=0.0, base=0,
                           pattern=[[-1, P]], channel_multiplier=1).then_inc(self.consts, 1)
        pool.affine_select(out=self.mask[:, :], in_=self.mask[:, :], compare_op=ALU.is_ge, fill=0.0, base=0,
                           pattern=[[1, 512]], channel_multiplier=-64).then_inc(self.consts, 1)
        pool.wait_ge(self.consts, 4)
        pool.affine_select(out=self.mask[:, :], in_=self.mask[:, :], compare_op=ALU.is_ge, fill=0.0, base=63,
                           pattern=[[-1, 512]], channel_multiplier=64).then_inc(self.consts, 1)
        pool.wait_ge(self.tables_in, 32)

    def load_v(self, pool, b, c):
        pool.wait_ge(self.v_used, b * self.PAGES + (c + 1))
        page = pool.value_load(self.pages[0:1, ds(b * self.PAGES + c, 1)], min_val=0, max_val=639)
        pool.dma_start(self.vt[:, c % self.VR], self.values[:, ds(page, 1), :]).then_inc(self.v_in[c % self.VR], 16)

    def load_q(self, v, b):
        v.wait_ge(self.q_in, b * 16 + 16)

    def score(self, v, b, c):
        r = c % self.KR
        keys = self.kt[:, r].rearrange("p (a n) -> p a n", a=self.KC)
        q = self.q[:, :].rearrange("p (a n) -> p a n", a=1).to_broadcast([P, self.KC, 512])
        if c == 0:
            v.wait_ge(self.biased, b)
        v.wait_ge(self.k_in[r], b * 256 + (c // self.KR + 1) * 32)
        v.tensor_tensor(keys, keys, q, ALU.mult).then_inc(self.k_times_q, 1)
        v.wait_ge(self.k_times_q, b * 32 + (c + 1))
        v.tensor_reduce(self.z[:, c * 16:(c + 1) * 16], self.kt[:, r].rearrange("p (h d) -> p h d", d=64), AX.X,
                        ALU.add).then_inc(self.scored, 1)

    def add_bias(self, v, b):
        v.wait_ge(self.scored, b * 32 + 32 + self.KR)
        v.wait_ge(self.weighted, b + 1)
        view = lambda t: t[:, :].rearrange("p (g h) -> p g h", h=NS)
        v.scalar_tensor_tensor(out=view(self.zb), in0=view(self.z), scalar=0.125,
                               in1=self.bias[:, :].rearrange("p (a h) -> p a h", a=1).to_broadcast([P, self.PAGES, NS]),
                               op0=ALU.mult, op1=ALU.add).then_inc(self.biased, 1)

    def softplus(self, v, b):
        v.wait_ge(self.kept, b * 3 + 3)
        v.scalar_tensor_tensor(out=self.e[:, :], in0=self.zb[:, :], scalar=0.0, in1=self.e[:, :], op0=ALU.max,
                               op1=ALU.add).then_inc(self.softplus_done, 1)

    def later_pages(self, v, b):
        v.wait_ge(self.sums, b * 2 + 2)
        last = 8 * (self.PAGES - 1)
        v.memset(self.e[:, last:], 0.0).then_inc(self.later, 1)
        for h in range(NS):
            v.tensor_tensor_scan(self.e[:, last - 8 + h::-8], self.k.ones[:, 0:self.PAGES - 1],
                                 self.k.ps[7][:, last + h:8 + h - 1:-8] if h else self.k.ps[7][:, last:7:-8],
                                 0.0, ALU.mult, ALU.add).then_inc(self.later, 1)

    def log_weights(self, v, b):
        v.tensor_tensor(self.zb[:, :], self.zb[:, :], self.k.ps[6][:, :], ALU.subtract).then_inc(self.logw, 1)
        v.wait_ge(self.logw, b * 2 + 2)
        v.wait_ge(self.later, b * 9 + 9)
        v.tensor_tensor(self.zb[:, :], self.zb[:, :], self.e[:, :], ALU.subtract).then_inc(self.logw, 1)

    def own_heads(self, v, b):
        v.wait_ge(self.v_used, b * self.PAGES + self.PAGES + self.VR)
        v.wait_ge(self.columns_done, b + 1)
        v.wait_ge(self.consts, 5)
        v.tensor_tensor(self.own[:, :], self.k.ps[6][0:NS, :], self.mask[:, :], ALU.mult).then_inc(self.own_done, 1)

    def log_keep(self, act, b):
        act.wait_ge(self.biased, b + 1)
        act.wait_ge(self.logw, b * 2 + 1)
        act.activation(self.e[:, :], self.zb[:, :], ACT.Abs).then_inc(self.kept, 1)
        act.wait_ge(self.kept, b * 3 + 1)
        act.activation(self.e[:, :], self.e[:, :], ACT.Exp, scale=-1.0).then_inc(self.kept, 1)
        act.wait_ge(self.kept, b * 3 + 2)
        act.activation(self.e[:, :], self.e[:, :], ACT.Ln, bias=1.0).then_inc(self.kept, 1)

    def weights(self, act, b):
        act.wait_ge(self.logw, b * 2 + 3)
        act.wait_ge(self.v_used, b * self.PAGES + self.VR)
        act.activation(self.w[:, :], self.zb[:, :], ACT.Exp).then_inc(self.weighted, 1)

    def store(self, act, b):
        act.wait_ge(self.columns_done, b + 2)
        act.activation(self.k.osT[:, :, ds(b, 1)], self.k.ps[7][:, 0:4].rearrange("p (k a) -> p k a", a=1),
                       ACT.Copy).then_inc(self.stored, 1)

    def page_sums(self, pe, b):
        pe.wait_ge(self.softplus_done, b + 1)
        pe.wait_ge(self.stored, b + 1)
        pe.wait_ge(self.own_done, b + 1)
        pe.wait_ge(self.consts, 5)
        pe.matmul(self.k.ps[7][:, :], self.k.ones[:, :], self.e[:, :], start=True, stop=True).then_inc(self.sums, 1)
        pe.matmul(self.k.ps[6][:, :], self.tri[:, :], self.e[:, :], start=True, stop=True).then_inc(self.sums, 1)

    def weigh(self, pe, b, part):
        if part == 0:
            pe.wait_ge(self.weighted, b + 2)
        for j in range(8):
            g = part * 8 + j
            pe.wait_ge(self.v_in[j], b * 128 + (part + 1) * 16)
            pe.matmul(self.k.ps[6][0:NS, :], self.w[:, g * 8:(g + 1) * 8], self.vt[:, j], start=g == 0,
                      stop=g == self.PAGES - 1).then_inc(self.v_used, 1)

    def columns(self, pe, b):
        pe.wait_ge(self.own_done, b + 2)
        for j in range(4):
            i = pe.matmul(self.k.ps[7][:, j:j + 1], self.own[:, j * P:(j + 1) * P], self.k.ones[0:NS, 0:1],
                          start=True, stop=True)
        i.then_inc(self.columns_done, 1)


class Kernel:
    def __init__(self, nc, a, o):
        self.nc, self.a, self.o = nc, a, o
        self.ctx = ExitStack()
        self.cursor = (nc.sbuf_base + 31) // 32 * 32
        self.persistent()

    def sem(self, name):
        return self.nc.alloc_semaphore(name=name)

    def at(self, name, shape, dt=F32):
        size = 4
        for n in shape[1:]:
            size *= n
        t = self.nc.alloc_sbuf_tensor_at(name, shape, dt, offset=self.cursor)
        self.cursor += (size + 31) // 32 * 32
        return t

    def persistent(self):
        nc = self.nc
        self.xT = self.at("xT", [P, KD, NT])
        self.ring_start = self.cursor
        self.raw = self.at("raw", [P, RAW_RING, D])
        self.whi = [self.at(f"whi{s}", [P, D], F32R) for s in range(W_RING)]
        self.wlo = [self.at(f"wlo{s}", [P, D], F32R) for s in range(W_RING)]
        self.ring_end = self.cursor
        self.ident = self.at("ident", [P, P])
        self.ones = self.at("ones", [P, P])
        self.gains = self.at("gains", [P, 7, KD])
        self.b_glu = self.at("b_glu", [P, 4])
        self.osT = self.at("osT", [P, 4, NS])
        self.psum = self.ctx.enter_context(nc.psum_tensor("banks", [P, 8 * 512], F32))
        self.ps = [self.psum[:, b * 512:(b + 1) * 512] for b in range(8)]
        self.arena = self.cursor
        self.ssm_angle, self.ssm_ck, self.ssm_gt, self.ssm_states = 13, 60, 66, 238
        self.qs_dram = nc.dram_tensor("qs_scratch", [NS, 512], F32).ap()
        self.xq_dram = nc.dram_tensor("xq_scratch", [NS, D], F32).ap()
        self.us_dram = nc.dram_tensor("us_scratch", [NS, 512], F32).ap()

    def samples_ahead(self):
        nc, a, o, ps = self.nc, self.a, self.o, self.ps
        self.cursor = self.arena
        CH = 256
        RING = 6
        wide = self.at("a_wide", [P, RING, 2048])
        xp = self.at("a_xp", [P, 4, D])
        xs = self.at("a_xs", [NS, D])
        gbc = self.at("a_gbc", [NS, 2, D])
        hs = self.at("a_hs", [NS, D])
        x1 = self.at("a_x1", [NS, D])
        gs = self.at("a_gs", [NS, FF])
        sg = self.at("a_sg", [NS, 2, CH])
        proj = self.at("a_proj", [NS, 2048])
        hT = self.at("a_hT", [P, 2, KD, NS])
        gT = self.at("a_gT", [P, 22, NS])
        st = self.at("a_st", [NS, 8])

        nff = FF // CH
        units = []
        for c in range(nff):
            for w in ("w_ffn1_gate", "w_ffn1_up"):
                units.append(a[w].rearrange("(k p) n -> p k n", p=P)[:, :, c * CH:(c + 1) * CH])
        for c in range(nff):
            units.append(a["w_ffn1_down"].rearrange("(f p) n -> p f n", p=P)[:, 2 * c:2 * c + 2, :])
        for c in range(8):
            units.append(a["w_in"].rearrange("(k p) n -> p k n", p=P)[:, :, c * CH:(c + 1) * CH])
        DOWN0, IN0 = 2 * nff, 3 * nff

        consts = self.sem("a_consts")
        small_in = self.sem("a_small_in")
        gains_in = self.sem("a_gains_in")
        xp_in = [self.sem(f"a_xp_in{j}") for j in range(4)]
        landed = [self.sem(f"a_landed{r}") for r in range(RING)]
        used = self.sem("a_used")
        act_done = self.sem("a_act")
        h_done = self.sem("a_h")
        dve = self.sem("a_dve")
        hT_ps = self.sem("a_hT_ps")
        hT_sb = self.sem("a_hT_sb")
        xt_ps = self.sem("a_xt_ps")
        xt_sb = self.sem("a_xt_sb")
        silu = self.sem("a_silu")
        g_done = self.sem("a_g")
        gT_ps = self.sem("a_gT_ps")
        gT_sb = self.sem("a_gT_sb")
        x1_done = self.sem("a_x1")
        in_sb = self.sem("a_in_sb")
        xsT_ps = self.sem("a_xsT_ps")
        stores = self.sem("a_stores")

        def wide_view(n):
            k = 2 if DOWN0 <= n < IN0 else 8
            return wide[:, n % RING].rearrange("p (k m) -> p k m", k=k)

        GAINS = ["g_ffn1", "g_mix", "g_xattn", "g_mem", "g_ffn2", "g_final"]
        with nc.Block() as block:
            @block.sync
            def _(sp):
                sp.dma_start(xs[:, :], a["x_sample"]).then_inc(small_in, 16)
                for j, g in enumerate(("g_ffn1", "g_mix")):
                    sp.dma_start(gbc[:, j], a[g].rearrange("(a n) -> a n", a=1).to_broadcast([NS, D])).then_inc(small_in, 16)

                def load(n):
                    if n >= RING:
                        sp.wait_ge(used, n - RING + 1)
                    sp.dma_start(wide_view(n), units[n]).then_inc(landed[n % RING], 16)

                for n in range(len(units)):
                    load(n)
                    if n < 16 and n % 2:
                        tb = n // 2
                        if tb >= 4:
                            sp.wait_ge(xt_ps, 2 * (tb - 4) + 2)
                        sp.dma_start(xp[:, tb % 4], a["x_prompt"][tb * P:(tb + 1) * P, :]).then_inc(xp_in[tb % 4], 16)
                sp.wait_ge(in_sb, 8)
                sp.dma_start(o["k_sample"], proj[:, 512:1024]).then_inc(stores, 16)
                sp.dma_start(o["v_sample"], proj[:, 1024:1536]).then_inc(stores, 16)
                sp.dma_start(self.qs_dram, proj[:, 0:512]).then_inc(stores, 16)
                sp.dma_start(self.us_dram, proj[:, 1536:2048]).then_inc(stores, 16)
                sp.wait_ge(stores, 64)

            @block.gpsimd
            def _(pool):
                pool.memset(self.ones[:, :], 1.0).then_inc(consts, 1)
                pool.memset(self.ident[:, :], 0.0).then_inc(consts, 1)
                pool.wait_ge(consts, 2)
                pool.affine_select(out=self.ident[:, :], in_=self.ident[:, :], compare_op=ALU.not_equal,
                                   fill=1.0, base=0, pattern=[[-1, P]], channel_multiplier=1).then_inc(consts, 1)
                for j, g in enumerate(GAINS):
                    pool.dma_start(self.gains[:, j], a[g].rearrange("(k p) -> p k", p=P),
                                   allow_slow_non_contiguous=True).then_inc(gains_in, 16)
                for j, g in enumerate(("g_sb_out", "g_ssm_out")):
                    pool.dma_start(self.gains[:, 6, 4 * j:4 * j + 4], a[g].rearrange("(k p) -> p k", p=P),
                                   allow_slow_non_contiguous=True).then_inc(gains_in, 16)
                pool.dma_start(self.b_glu[:, :], a["b_glu"].rearrange("(k p) -> p k", p=P),
                               allow_slow_non_contiguous=True).then_inc(gains_in, 16)
                pool.wait_ge(gains_in, 16 * 9)

            @block.scalar
            def _(act):
                n_act = [0]

                def link(i):
                    n_act[0] += 1
                    i.then_inc(act_done, 1)
                    act.wait_ge(act_done, n_act[0])

                def norm_stats(src):
                    link(act.activation(hs[:, :], src, ACT.Square, accum_out=st[:, 0:1]))
                    link(act.activation(st[:, 1:2], st[:, 0:1], ACT.Copy, scale=1.0 / D, bias=EPS))
                    link(act.activation(st[:, 2:3], st[:, 1:2], ACT.Sqrt))

                act.wait_ge(small_in, 16 * 3)
                norm_stats(xs[:, :])

                def turn_prompt(tb):
                    act.wait_ge(xt_ps, 2 * tb + 1)
                    act.activation(self.xT[:, 0:4, tb * P:(tb + 1) * P],
                                   ps[4][:, :].rearrange("p (k m) -> p k m", k=4), ACT.Copy).then_inc(xt_sb, 1)

                for c in range(nff):
                    act.wait_ge(used, 2 * c + 1)
                    if c >= 2:
                        act.wait_ge(g_done, c - 1)
                    act.activation(sg[:, c % 2], ps[c % 2][0:NS, 0:CH], ACT.Silu).then_inc(silu, 1)
                    if c < 8:
                        turn_prompt(c)
                act.wait_ge(x1_done, 2)
                norm_stats(x1[:, :])
                for c in range(8):
                    act.wait_ge(used, IN0 + c + 1)
                    act.activation(proj[:, c * CH:(c + 1) * CH], ps[c % 4][0:NS, 0:CH], ACT.Copy).then_inc(in_sb, 1)

            @block.vector
            def _(dve_):
                v = dve_
                n_dve = [0]

                def normalise(src, j, stats):
                    v.wait_ge(act_done, stats)
                    v.reciprocal(st[:, 3:4], st[:, 2:3]).then_inc(dve, 1)
                    n_dve[0] += 1
                    v.wait_ge(dve, n_dve[0])
                    v.scalar_tensor_tensor(out=hs[:, :], in0=src, scalar=st[:, 3:4], in1=gbc[:, j],
                                           op0=ALU.mult, op1=ALU.mult).then_inc(h_done, 1)
                    v.wait_ge(hT_ps, j + 1)
                    v.tensor_copy(hT[:, j], ps[6][:, 0:KD * NS].rearrange("p (k m) -> p k m", k=KD)).then_inc(hT_sb, 1)

                normalise(xs[:, :], 0, 3)
                for c in range(nff):
                    v.wait_ge(used, 2 * c + 2)
                    v.wait_ge(silu, c + 1)
                    v.tensor_tensor(gs[:, c * CH:(c + 1) * CH], sg[:, c % 2], ps[2 + c % 2][0:NS, 0:CH],
                                    ALU.mult).then_inc(g_done, 1)
                    if c < 8:
                        v.wait_ge(xt_ps, 2 * c + 2)
                        v.tensor_copy(self.xT[:, 4:8, c * P:(c + 1) * P],
                                      ps[5][:, :].rearrange("p (k m) -> p k m", k=4)).then_inc(xt_sb, 1)
                v.wait_ge(gT_ps, 1)
                v.tensor_copy(gT[:, :, :], ps[7][:, 0:22 * NS].rearrange("p (k m) -> p k m", k=22)).then_inc(gT_sb, 1)
                for half in range(2):
                    v.wait_ge(used, IN0)
                    v.scalar_tensor_tensor(out=x1[:, half * 512:(half + 1) * 512], in0=ps[4 + half][0:NS, :], scalar=0.5,
                                           in1=xs[:, half * 512:(half + 1) * 512], op0=ALU.mult,
                                           op1=ALU.add).then_inc(x1_done, 1)
                normalise(x1[:, :], 1, 6)
                v.wait_ge(xsT_ps, 1)
                v.tensor_copy(self.xT[:, :, NP:NT], ps[7][:, 0:KD * NS].rearrange("p (k m) -> p k m", k=KD)).then_inc(dve, 1)

            @block.tensor
            def _(pe):
                pe.wait_ge(consts, 3)

                def turn(src, bank, m, count):
                    for k in range(count):
                        i = pe.transpose(ps[bank][:, k * m:(k + 1) * m], src[:, k * P:(k + 1) * P], self.ident[0:m, 0:m])
                    return i

                def turn_prompt(tb):
                    pe.wait_ge(xp_in[tb % 4], 16 * (tb // 4 + 1))
                    if tb:
                        pe.wait_ge(xt_sb, 2 * tb)
                    for half in range(2):
                        turn(xp[:, tb % 4, half * 512:(half + 1) * 512], 4 + half, P, 4).then_inc(xt_ps, 1)

                pe.wait_ge(h_done, 1)
                turn(hs, 6, NS, KD).then_inc(hT_ps, 1)
                pe.wait_ge(hT_sb, 1)
                for c in range(nff):
                    for j in range(2):
                        n = 2 * c + j
                        pe.wait_ge(landed[n % RING], 16 * (n // RING + 1))
                        if c >= 2:
                            pe.wait_ge(g_done, c - 1)
                        for k in range(KD):
                            i = pe.matmul(ps[2 * j + c % 2][0:NS, 0:CH], hT[:, 0, k], wide_view(n)[:, k],
                                          start=k == 0, stop=k == KD - 1)
                        i.then_inc(used, 1)
                    if c < 8:
                        turn_prompt(c)
                pe.wait_ge(g_done, nff)
                turn(gs, 7, NS, 22).then_inc(gT_ps, 1)
                pe.wait_ge(gT_sb, 1)
                pe.wait_ge(xt_sb, 16)
                for f in range(22):
                    n = DOWN0 + f // 2
                    if f % 2 == 0:
                        pe.wait_ge(landed[n % RING], 16 * (n // RING + 1))
                    for half in range(2):
                        i = pe.matmul(ps[4 + half][0:NS, :], gT[:, f], wide_view(n)[:, f % 2, half * 512:(half + 1) * 512],
                                      start=f == 0, stop=f == 21)
                    if f % 2:
                        i.then_inc(used, 1)
                pe.wait_ge(x1_done, 2)
                turn(x1, 7, NS, KD).then_inc(xsT_ps, 1)
                pe.wait_ge(h_done, 2)
                turn(hs, 6, NS, KD).then_inc(hT_ps, 1)
                pe.wait_ge(hT_sb, 2)
                for c in range(8):
                    n = IN0 + c
                    pe.wait_ge(landed[n % RING], 16 * (n // RING + 1))
                    if c >= 4:
                        pe.wait_ge(in_sb, c - 3)
                    for k in range(KD):
                        i = pe.matmul(ps[c % 4][0:NS, 0:CH], hT[:, 1, k], wide_view(n)[:, k], start=k == 0, stop=k == KD - 1)
                    i.then_inc(used, 1)

    def ffn(self, name, tiles, gate, up, down, gain, decode=False):
        nc, a, ps = self.nc, self.a, self.ps
        self.cursor = self.arena
        T = len(tiles)
        N = tiles[-1][0] + tiles[-1][1]
        GROUPS = FF // 256
        TILES_DOWN = KD * T
        hhi = self.at(f"{name}_hhi", [P, KD, N], F32R)
        hlo = self.at(f"{name}_hlo", [P, KD, N], F32R)
        ghi = self.at(f"{name}_ghi", [P, 2, N], F32R)
        glo = self.at(f"{name}_glo", [P, 2, N], F32R)
        sg = self.at(f"{name}_silu", [P, T, tiles[0][1]])
        gt = self.at(f"{name}_g", [P, T, tiles[0][1]])
        dt_ = self.at(f"{name}_down", [P, T, tiles[0][1]])
        DR = 2
        GATE = list(range(T))
        UP = list(range(T, 2 * T))
        DOWN = [2 * T, 2 * T + 1]

        d_start = self.cursor
        if decode:
            d = Decode(self, name)
            aux = nc.alloc_sbuf_tensor_at(f"{name}_aux", [P, 2, 512], F32, offset=d_start + (16384 + 16384 + 2048))
        else:
            aux = self.at(f"{name}_aux", [P, 2, 512])
        w = Stream(self, name)
        norm = Norm(self, f"{name}_n", tiles, lambda k, t0, n: self.xT[:, k, t0:t0 + n], KD,
                    lambda k: self.gains[:, gain, k:k + 1], hhi, hlo, sg, gt, dt_, aux, GATE)
        gate_ps = self.sem(f"{name}_gate_ps")
        up_ps = self.sem(f"{name}_up_ps")
        silu = self.sem(f"{name}_silu")
        g_done = self.sem(f"{name}_g_done")
        g_hi = self.sem(f"{name}_g_hi")
        g_lo = self.sem(f"{name}_g_lo")
        down_ps = self.sem(f"{name}_down_ps")
        drained = self.sem(f"{name}_drained")
        added = self.sem(f"{name}_added")

        def gate_unit(wt, i, f):
            return wt.rearrange("(k p) n -> p k n", p=P)[:, :, ds(i * 256 + f * P, P)]

        def down_unit(i, f):
            return down.rearrange("(b p) n -> p b n", p=P)[:, ds(i * 2 + f, 1), :]

        def groups(eng, body):
            if decode:
                body(0, True, False, False)
                with eng.Fori(1, NS) as i:
                    body(i, True, True, False)
                body(NS, False, True, False)
                body(NS + 1, False, False, False)
            else:
                with eng.Fori(0, GROUPS - 1) as i:
                    body(i, False, False, False)
            body(GROUPS - 1, False, False, True)

        with nc.Block() as block:
            @block.sync
            def _(sp):
                def body(i, K, V, last):
                    def unit(c, j, e):
                        if j is None or isinstance(j, int) and j > GROUPS - 1:
                            return
                        if c < 4:
                            w.load(sp, j * 6 + c, c, gate_unit((gate, up)[c % 2], j, c // 2), 8)
                        else:
                            w.load(sp, j * 6 + c, c, down_unit(j, c - 4), 1)

                    def K_(lo_, hi_):
                        if K:
                            for c in range(lo_, hi_):
                                d.load_k(sp, i, c)
                    nxt = i + 1
                    K_(0, 4)
                    unit(4, i, 0)
                    K_(4, 8)
                    unit(5, i, 0)
                    K_(8, 16)
                    unit(0, nxt, 0) if not last else None
                    K_(16, 24)
                    unit(1, nxt, 0) if not last else None
                    K_(24, 28)
                    unit(2, nxt, 0) if not last else None
                    K_(28, 32)
                    unit(3, nxt, 0) if not last else None
                if decode:
                    d.load_tables(sp)
                for c in range(4):
                    w.load(sp, c, c, gate_unit((gate, up)[c % 2], 0, c // 2), 8)
                groups(sp, body)

            @block.gpsimd
            def _(pool):
                pool.sem_inc(added, DR)

                def body(i, K, V, last):
                    def V_(lo_, hi_):
                        if V:
                            for c in range(lo_, hi_):
                                d.load_v(pool, i - 1, c)
                    V_(0, 40)
                    for m in range(TILES_DOWN):
                        if m in (4, 8, 12):
                            V_(8 * (m // 4 + 4), 8 * (m // 4 + 5))
                        t, k = divmod(m, KD)
                        t0, n = tiles[t]
                        x = self.xT[:, k, t0:t0 + n]
                        pool.wait_ge(drained, i * TILES_DOWN + (m + 3))
                        pool.tensor_tensor(x, x, dt_[:, m % DR, 0:n], ALU.add).then_inc(added, 1)
                if decode:
                    d.prepare(pool)
                groups(pool, body)

            @block.scalar
            def _(act):
                act.sem_inc(silu, T)
                act.sem_inc(drained, 2)
                if decode:
                    act.sem_inc(d.weighted, 1)
                    act.sem_inc(d.stored, 1)
                w.hi(act, 0, 0, 1)
                w.hi(act, 1, 1, 1)
                norm.act(act)

                def silus(i, f):
                    for t, (t0, n) in enumerate(tiles):
                        act.wait_ge(gate_ps, i * (2 * T) + (f * T + t + 1))
                        act.wait_ge(g_done, i * (2 * T) + (f * T + t + 1))
                        act.activation(sg[:, t, 0:n], ps[GATE[t]][:, 0:n], ACT.Silu).then_inc(silu, 1)

                def g_his(i, f):
                    for t, (t0, n) in enumerate(tiles):
                        act.wait_ge(g_done, i * (2 * T) + (f * T + t + 1 + T))
                        act.wait_ge(down_ps, i * TILES_DOWN + 1)
                        act.activation(ghi[:, f, t0:t0 + n], gt[:, t, 0:n], ACT.Copy).then_inc(g_hi, 1)

                def body(i, K, V, last):
                    w.hi(act, i * 6 + 2, 2, i * 3 + 2, down_ps, i * TILES_DOWN + 1)
                    if V:
                        d.log_keep(act, i - 1)
                    silus(i, 0)
                    w.hi(act, i * 6 + 3, 3, i * 3 + 2, gate_ps, i * (2 * T) + T)
                    g_his(i, 0)
                    w.hi(act, i * 6 + 4, 4, i * 3 + 3, up_ps, i * (2 * T) + T)
                    if V:
                        d.weights(act, i - 1)
                    silus(i, 1)
                    w.hi(act, i * 6 + 5, 5, i * 3 + 3, gate_ps, i * (2 * T) + 2 * T)
                    g_his(i, 1)
                    if not last:
                        w.hi(act, i * 6 + 6, 0, i * 3 + 4, up_ps, i * (2 * T) + 2 * T)
                    for m in range(TILES_DOWN):
                        n = tiles[m // KD][1]
                        act.wait_ge(down_ps, i * TILES_DOWN + (m + 2))
                        act.wait_ge(added, i * TILES_DOWN + (m + 1))
                        act.activation(dt_[:, m % DR, 0:n], ps[DOWN[m % 2]][:, 0:n], ACT.Copy,
                                       scale=0.5).then_inc(drained, 1)
                    if V:
                        d.store(act, i - 1)
                    if not last:
                        w.hi(act, i * 6 + 7, 1, i * 3 + 4, down_ps, i * TILES_DOWN + (TILES_DOWN + 1))
                groups(act, body)

            @block.vector
            def _(v):
                w.credits_dve(v)
                v.sem_inc(g_done, T)
                v.sem_inc(g_lo, T)
                w.lo(v, 0, 0)
                w.lo(v, 1, 1)
                if decode:
                    v.sem_inc(d.scored, d.KR)
                    v.sem_inc(d.logw, 1)
                    v.sem_inc(d.own_done, 1)
                norm.dve(v)

                def gs(i, f):
                    for t, (t0, n) in enumerate(tiles):
                        v.wait_ge(up_ps, i * (2 * T) + (f * T + t + 1))
                        v.wait_ge(silu, i * (2 * T) + (f * T + t + 1 + T))
                        v.wait_ge(g_lo, i * (2 * T) + (f * T + t + 1))
                        v.tensor_tensor(gt[:, t, 0:n], sg[:, t, 0:n], ps[UP[t]][:, 0:n], ALU.mult).then_inc(g_done, 1)
                    for t, (t0, n) in enumerate(tiles):
                        v.wait_ge(g_hi, i * (2 * T) + (f * T + t + 1))
                        v.tensor_tensor(glo[:, f, t0:t0 + n], gt[:, t, 0:n], ghi[:, f, t0:t0 + n].bitcast(F32),
                                        ALU.subtract).then_inc(g_lo, 1)

                def body(i, K, V, last):
                    def K_(lo_, hi_):
                        if K:
                            for c in range(lo_, hi_):
                                d.score(v, i, c)
                    if V:
                        d.add_bias(v, i - 1)
                    w.lo(v, i * 6 + 2, 2)
                    if K:
                        d.load_q(v, i)
                    K_(0, 2)
                    if V:
                        d.softplus(v, i - 1)
                    K_(2, 4)
                    w.lo(v, i * 6 + 3, 3)
                    if V:
                        d.later_pages(v, i - 1)
                    K_(4, 8)
                    gs(i, 0)
                    w.lo(v, i * 6 + 4, 4)
                    if V:
                        d.log_weights(v, i - 1)
                    K_(8, 16)
                    w.lo(v, i * 6 + 5, 5)
                    K_(16, 24)
                    gs(i, 1)
                    if not last:
                        w.lo(v, i * 6 + 6, 0)
                    K_(24, 32)
                    if V:
                        d.own_heads(v, i - 1)
                    if not last:
                        w.lo(v, i * 6 + 7, 1)
                groups(v, body)

            @block.tensor
            def _(pe):
                pe.sem_inc(down_ps, 1)
                if decode:
                    pe.sem_inc(d.columns_done, 1)
                norm.pe(pe)
                norm.ready(pe)

                def unit(i, c):
                    f, is_up = divmod(c, 2)
                    w.ready(pe, i * 6 + c)
                    for t, (t0, n) in enumerate(tiles):
                        pe.wait_ge(g_done if is_up else silu, i * (2 * T) + (f * T + t + 1))
                        bank = (UP if is_up else GATE)[t]
                        for k in range(KD):
                            last = three_passes(pe, ps[bank][:, 0:n], self.whi[c % 3][:, k * P:(k + 1) * P],
                                                self.wlo[c % 3][:, k * P:(k + 1) * P], hhi[:, k, t0:t0 + n],
                                                hlo[:, k, t0:t0 + n], k == 0, k == KD - 1)
                        last.then_inc(up_ps if is_up else gate_ps, 1)
                        yield

                def body(i, K, V, last):
                    parts = iter(range(8))

                    def cache_values():
                        if V:
                            d.weigh(pe, i - 1, next(parts))
                    for _ in unit(i, 0):
                        pass
                    if V:
                        d.page_sums(pe, i - 1)
                    for _ in unit(i, 1):
                        pass
                    for c in (2, 3):
                        for _ in unit(i, c):
                            cache_values()
                    w.ready(pe, i * 6 + 4)
                    w.ready(pe, i * 6 + 5)
                    for m in range(TILES_DOWN):
                        t, k = divmod(m, KD)
                        t0, n = tiles[t]
                        if k == 0:
                            pe.wait_ge(g_lo, i * (2 * T) + (2 * T + t + 1))
                        pe.wait_ge(drained, i * TILES_DOWN + (m + 1))
                        for f in range(2):
                            j = three_passes(pe, ps[DOWN[m % 2]][:, 0:n], self.whi[1 + f][:, k * P:(k + 1) * P],
                                             self.wlo[1 + f][:, k * P:(k + 1) * P], ghi[:, f, t0:t0 + n],
                                             glo[:, f, t0:t0 + n], f == 0, f == 1)
                        j.then_inc(down_ps, 1)
                        if m % 4 == 3 and m < 16:
                            cache_values()
                    if V:
                        d.columns(pe, i - 1)
                groups(pe, body)

    def project_in(self):
        nc, a = self.nc, self.a
        self.cursor = self.arena
        self.qkvu = self.at("qkvu", [P, 16, NP])
        self.after_qkvu = self.cursor
        hhi = self.at("in_hhi", [P, KD, NP], F32R)
        hlo = self.at("in_hlo", [P, KD, NP], F32R)
        self.cursor = self.after_qkvu - 4 * 4096
        square, tmp, root, aux = (self.at(f"in_{n}", [P, 2, 512]) for n in ("square", "tmp", "root", "aux"))
        norm = Norm(self, "in_n", PROMPT_TILES, lambda k, t0, n: self.xT[:, k, t0:t0 + n], KD,
                    lambda k: self.gains[:, 1, k:k + 1], hhi, hlo, square, tmp, root, aux, [0, 1])
        proj = Project(self, "in", 16, lambda n, c, half: a["w_in"].rearrange("(k p) n -> p k n", p=P)[:, :, ds(n * P, P)],
                       hhi, hlo, PROMPT_TILES, [0, 1, 2, 3])
        with nc.Block() as block:
            @block.sync
            def _(sp):
                proj.sp(sp)

            @block.scalar
            def _(act):
                proj.credits_drain(act)
                norm.act(act)

                def drain(n, c, t, t0, size, bank):
                    act.activation(self.qkvu[:, ds(n, 1), t0:t0 + size],
                                   self.ps[bank][:, 0:size].rearrange("p (a n) -> p a n", a=1), ACT.Copy).then_inc(proj.drained, 1)
                proj.act(act, drain)

            @block.vector
            def _(v):
                proj.credits_dve(v)
                norm.dve(v)
                proj.dve(v)

            @block.tensor
            def _(pe):
                norm.pe(pe)
                norm.ready(pe)
                proj.pe(pe)

    def attention(self):
        nc, a, o, ps = self.nc, self.a, self.o, self.ps
        self.cursor = self.after_qkvu
        self.oT = self.at("oT", [P, 4, NT])
        qc, kc, vc = (self.at(f"at_{n}", [P, NP]) for n in ("q", "k", "v"))
        ktm, vtm = (self.at(f"at_{n}", [P, 8, P]) for n in ("k_rows", "v_rows"))
        SLOTS = 4
        z = self.at("at_z", [P, SLOTS, NP])
        w = self.at("at_w", [P, SLOTS, NP])
        e = self.place("at_e", [P, SLOTS, NP], 0, ring=True)
        wT = self.at("at_wT", [P, 2, NP])
        bias = self.at("at_bias", [P, 8])
        later = self.place("at_later", [P, P], 16, ring=True)
        bc = self.at("at_bias_pair", [P, 2])
        UNITS = 16
        BEHIND = 2
        keys = lambda u: (u % 8 + 1) * P
        MASKED = -1e30
        LARGEST = 1e38

        names = ("bias_in", "consts", "copied", "rows_ps", "k_rows", "v_rows", "stores", "z_ps", "z_sb", "exped",
                 "cut", "logged", "soft", "scanned", "subtracted", "weighted", "turned", "wT", "pv", "out_sb")
        S = {n: self.sem(f"at_{n}") for n in names}

        def pairs_of_heads(eng, body, rest):
            body(0, None)
            with eng.Fori(1, 4) as j:
                body(j, j - 1)
            rest(3)

        def backs(j, back):
            for p in range(BEHIND):
                back(j, UNITS + 2 * (p - BEHIND))

        with nc.Block() as block:
            @block.sync
            def _(sp):
                sp.dma_start(bias[:, :], a["sb_bias"].rearrange("(a n) -> a n", a=1).to_broadcast([P, 8])).then_inc(S["bias_in"], 16)
                sp.sem_inc(S["stores"], 1)
                with sp.Fori(0, 4) as j:
                    for name, src, done in (("k_prompt", ktm, "k_rows"), ("v_prompt", vtm, "v_rows")):
                        sp.wait_ge(S[done], j * 2 + 2)
                        sp.dma_start(o[name].rearrange("(b p) n -> p b n", p=P)[:, :, ds(j * P, P)], src[:, :, :]).then_inc(S["stores"], 16)
                sp.wait_ge(S["stores"], 4 * 2 * 16 + 1)

            @block.gpsimd
            def _(pool):
                pool.sem_inc(S["subtracted"], SLOTS)
                pool.memset(later[:, :], 0.0).then_inc(S["consts"], 1)
                pool.wait_ge(S["consts"], 1)
                pool.affine_select(out=later[:, :], in_=later[:, :], compare_op=ALU.is_gt, fill=MASKED, base=0,
                                   pattern=[[-1, P]], channel_multiplier=1).then_inc(S["consts"], 1)

                def subtract(j, u):
                    n, t = keys(u), u % SLOTS
                    pool.wait_ge(S["scanned"], j * UNITS + (u + 1 + SLOTS))
                    pool.tensor_tensor(w[:, t, 0:n], z[:, t, 0:n], w[:, t, 0:n], ALU.subtract).then_inc(S["subtracted"], 1)

                with pool.Fori(0, 4) as j:
                    for u in range(UNITS):
                        subtract(j, u)

            @block.scalar
            def _(act):
                act.sem_inc(S["exped"], 2)
                act.sem_inc(S["out_sb"], 1)

                def exp(j, u):
                    n = keys(u)
                    act.wait_ge(S["z_ps"], j * UNITS + (u + 2))
                    act.wait_ge(S["scanned"], j * UNITS + (u + 1))
                    if u == 0:
                        act.wait_ge(S["copied"], j * 4 + 4)
                    act.activation(e[:, u % SLOTS, 0:n], self.psum[:, (u % 2) * 1024:(u % 2) * 1024 + n], ACT.Exp,
                                   bias=bc[:, u // 8:u // 8 + 1], scale=0.125).then_inc(S["exped"], 1)

                def log(j, u):
                    n = keys(u)
                    act.wait_ge(S["cut"], j * UNITS + (u + 1))
                    act.activation(e[:, u % SLOTS, 0:n], e[:, u % SLOTS, 0:n], ACT.Ln, bias=1.0).then_inc(S["logged"], 1)

                def weigh(j, u):
                    n = keys(u)
                    act.wait_ge(S["subtracted"], j * UNITS + (u + 1 + SLOTS))
                    act.activation(w[:, u % SLOTS, 0:n], w[:, u % SLOTS, 0:n], ACT.Exp).then_inc(S["weighted"], 1)

                def out(j):
                    act.wait_ge(S["pv"], j * UNITS + (UNITS + 2))
                    act.activation(self.oT[:, ds(j, 1), 0:NP], self.psum[:, 6 * 512:8 * 512].rearrange("p (a n) -> p a n", a=1),
                                   ACT.Copy).then_inc(S["out_sb"], 1)

                def body(j, before):
                    for p in range(UNITS // 2):
                        exp(j, 2 * p)
                        exp(j, 2 * p + 1)
                        if p == BEHIND:
                            if before is not None:
                                out(before)
                            act.wait_ge(S["rows_ps"], j * 4 + 3)
                            act.wait_ge(S["stores"], j * 32 + 1)
                            for half in range(2):
                                act.activation(ktm[:, 4 * half:4 * half + 4], ps[4 + half].rearrange("p (b n) -> p b n", b=4),
                                               ACT.Copy).then_inc(S["k_rows"], 1)
                        if p >= BEHIND:
                            weigh_two(j, 2 * (p - BEHIND))
                        elif before is not None:
                            weigh_two(before, UNITS + 2 * (p - BEHIND))
                        log(j, 2 * p)
                        log(j, 2 * p + 1)

                def weigh_two(j, u):
                    weigh(j, u)
                    weigh(j, u + 1)

                def rest(j):
                    backs(j, weigh_two)
                    out(j)
                pairs_of_heads(act, body, rest)

            @block.vector
            def _(v):
                v.sem_inc(S["z_sb"], 2)
                v.sem_inc(S["scanned"], SLOTS)
                v.sem_inc(S["wT"], 1)

                def scores(j, u):
                    n, t = keys(u), u % SLOTS
                    v.wait_ge(S["exped"], j * UNITS + (u + 3))
                    v.wait_ge(S["subtracted"], j * UNITS + (u + 1))
                    v.tensor_scalar(z[:, t, 0:n], self.psum[:, (u % 2) * 1024:(u % 2) * 1024 + n], 0.125,
                                    bc[:, u // 8:u // 8 + 1], ALU.mult, ALU.add).then_inc(S["z_sb"], 1)

                def cut(j, u):
                    n, t = keys(u), u % SLOTS
                    v.tensor_scalar(e[:, t, 0:n], e[:, t, 0:n], LARGEST, None, ALU.min).then_inc(S["cut"], 1)

                def scan(j, u):
                    n, t = keys(u), u % SLOTS
                    v.wait_ge(S["logged"], j * UNITS + (u + 1))
                    v.wait_ge(S["z_sb"], j * UNITS + (u + 3))
                    v.tensor_tensor(e[:, t, 0:n], e[:, t, 0:n], z[:, t, 0:n], ALU.max).then_inc(S["soft"], 1)
                    v.wait_ge(S["soft"], j * UNITS + (u + 1))
                    v.wait_ge(S["turned"], j * UNITS + (u + 1))
                    back = e[:, t, n - 1::-1]
                    v.tensor_tensor_scan(w[:, t, n - 1::-1], back, back, 0.0, ALU.add, ALU.max).then_inc(S["scanned"], 1)

                def take(j, u):
                    n = keys(u)
                    v.wait_ge(S["turned"], j * UNITS + (u + 1 + SLOTS))
                    v.wait_ge(S["pv"], j * UNITS + (u + 1))
                    v.tensor_copy(wT[:, u % 2, 0:n], self.psum[:, 4 * 512:4 * 512 + n]).then_inc(S["wT"], 1)

                v.wait_ge(S["bias_in"], 16)
                def take_two(j, u):
                    take(j, u)
                    take(j, u + 1)

                def body(j, before):
                    v.wait_ge(S["z_ps"], j * UNITS + 1)
                    v.wait_ge(S["rows_ps"], j * 4 + 1)
                    for k, dst in enumerate((qc, kc, vc)):
                        v.tensor_copy(dst[:, :].rearrange("p (a n) -> p a n", a=1), self.qkvu[:, ds(j + 4 * k, 1), :]).then_inc(S["copied"], 1)
                    v.wait_ge(S["z_sb"], j * UNITS + 2)
                    v.tensor_copy(bc[:, :], bias[:, ds(j * 2, 2)]).then_inc(S["copied"], 1)
                    v.wait_ge(S["copied"], j * 4 + 4)
                    for p in range(UNITS // 2):
                        for u in (2 * p, 2 * p + 1):
                            scores(j, u)
                            cut(j, u)
                        if p == BEHIND:
                            v.wait_ge(S["rows_ps"], j * 4 + 5)
                            v.wait_ge(S["stores"], j * 32 + 1)
                            v.wait_ge(S["pv"], j * UNITS + 2)
                            for half in range(2):
                                v.tensor_copy(vtm[:, 4 * half:4 * half + 4], ps[6 + half].rearrange("p (b n) -> p b n", b=4)).then_inc(S["v_rows"], 1)
                        of, first = (j, 2 * (p - BEHIND)) if p >= BEHIND else (before, UNITS + 2 * (p - BEHIND))
                        for i in range(2):
                            if of is not None:
                                take(of, first + i)
                            scan(j, 2 * p + i)
                pairs_of_heads(v, body, lambda j: backs(j, take_two))

            @block.tensor
            def _(pe):
                pe.sem_inc(S["z_ps"], 1)
                pe.sem_inc(S["rows_ps"], 1)
                pe.sem_inc(S["turned"], SLOTS)
                pe.sem_inc(S["pv"], 2)

                def scores(j, u):
                    h, qb = u // 8, u % 8
                    n = keys(u)
                    rows = slice(h * 64, h * 64 + 64)
                    pe.wait_ge(S["z_sb"], j * UNITS + (u + 1))
                    base = (u % 2) * 1024
                    for n0 in range(0, n, 512):
                        n1 = min(n, n0 + 512)
                        pe.matmul(self.psum[:, base + n0:base + n1], qc[rows, qb * P:(qb + 1) * P],
                                  kc[rows, n0:n1], start=True, stop=n1 < n)
                    i = pe.matmul(self.psum[:, base + n - P:base + n], self.ident[:, :], later[:, :], start=False, stop=True)
                    i.then_inc(S["z_ps"], 1)

                def turn(j, u):
                    pe.wait_ge(S["weighted"], j * UNITS + (u + 1))
                    pe.wait_ge(S["wT"], j * UNITS + (u + 1))
                    for kb in range(u % 8 + 1):
                        i = pe.transpose(self.psum[:, 2048 + kb * P:2048 + (kb + 1) * P], w[:, u % SLOTS, kb * P:(kb + 1) * P],
                                         self.ident[:, :])
                    i.then_inc(S["turned"], 1)

                def values(j, u):
                    h, qb = u // 8, u % 8
                    pe.wait_ge(S["wT"], j * UNITS + (u + 2))
                    for kb in range(qb + 1):
                        i = pe.matmul(self.psum[h * 64:h * 64 + 64, 3072 + qb * P:3072 + (qb + 1) * P],
                                      vtm[:, kb, h * 64:h * 64 + 64], wT[:, u % 2, kb * P:(kb + 1) * P],
                                      start=kb == 0, stop=kb == qb)
                    i.then_inc(S["pv"], 1)

                pe.wait_ge(S["consts"], 2)
                def rows(j):
                    pe.wait_ge(S["wT"], j * UNITS + 1)
                    pe.wait_ge(S["out_sb"], j + 1)
                    for src, bank in ((kc, 4), (vc, 6)):
                        for b in range(8):
                            i = pe.transpose(self.psum[:, bank * 512 + b * P:bank * 512 + (b + 1) * P], src[:, b * P:(b + 1) * P],
                                             self.ident[:, :])
                            if b % 4 == 3:
                                i.then_inc(S["rows_ps"], 1)
                    pe.wait_ge(S["k_rows"], j * 2 + 2)
                    pe.wait_ge(S["v_rows"], j * 2 + 2)

                def back(j, u, between=None):
                    turn(j, u)
                    if between:
                        scores(*between)
                    turn(j, u + 1)
                    values(j, u)
                    values(j, u + 1)

                def body(j, before):
                    pe.wait_ge(S["copied"], j * 4 + 3)
                    scores(j, 0)
                    scores(j, 1)
                    for p in range(UNITS // 2):
                        second = (j, 2 * p + 3) if 2 * p + 2 < UNITS else None
                        if second:
                            scores(j, 2 * p + 2)
                        if p == BEHIND:
                            rows(j)
                        if p >= BEHIND:
                            back(j, 2 * (p - BEHIND), second)
                        elif before is not None:
                            back(before, UNITS + 2 * (p - BEHIND), second)
                        elif second:
                            scores(*second)
                pairs_of_heads(pe, body, lambda j: backs(j, back))

    def ssm(self):
        nc, a, o, ps = self.nc, self.a, self.o, self.ps
        T, L, C, G = 16, 8, 16, 32
        XW, SW = P + 40, P + 1

        place = self.place
        gt = [place(f"s_gt{i}", [P, T, L, C], 8 * i) for i in range(2)]
        tmp = [place(f"s_tmp{i}", [P, 2304], 16 + 9 * i) for i in range(2)]
        braw = [place(f"s_b{i}", [P, T, C], 34 + i) for i in range(2)]
        craw = [place(f"s_c{i}", [P, T, C], 36 + i) for i in range(2)]
        crow = [place(f"s_crow{i}", [P, 2, P], 38 + i) for i in range(2)]
        dbc = place("s_dbc", [C, G, C], 45)
        kg = place("s_kg", [C, G, P], 48)
        ck = [place(f"s_ck{i}", [P, T, L + 1, C], 81 + 9 * i) for i in range(2)]
        gm = [place(f"s_gm{i}", [P, T, P], 99 + 8 * i) for i in range(2)]
        toep = place("s_toep", [P, G, P], 115)
        bb = [place(f"s_bb{i}", [P, T, C], 131 + i) for i in range(2)]
        sm = place("s_small", [P, 26, T], 133)
        smi = place("s_small_int", [P, T], 134.7, I32)
        pw = place("s_pw", [P, 2, L + 1, T], 134.8)
        rows = place("s_rows", [P, 4, P], 136)
        s0 = place("s_s0", [P, 2, NS, T], 138)
        sn = place("s_sn", [P, 4, NS, T], 139)
        U = place("s_U", [P, G, L, C], 99)
        Us = place("s_Us", [40, G, L, C], 115)
        X = place("s_X", [P, G, XW], 0, ring=True)
        t = [place(f"s_t{i}", [P, T * P], 8 * i) for i in range(4)]
        rot = [place(f"s_rot{i}", [P, T, P], 48 + 8 * i) for i in range(2)]
        half = [place(f"s_half{i}", [P, T * P // 2], 16 + 4 * i) for i in range(2)]
        S = [place("s_S0", [P, T, SW], 32), place("s_S1", [P, T, SW], 22, ring=True)]
        gsm = place("s_gsm", [P, 2, T, NS], 42)
        srows = place("s_srows", [P, 4, P], 43)
        yg = place("s_yg", [P, L, 512], 0)
        ys = place("s_ys", [NS, 512], 45)
        gT = place("s_gT", [P, 4, NT], 16)
        ghi = place("s_ghi", [P, 4, NT], 33, F32R)
        glo = place("s_glo", [P, 4, NT], 81, F32R)
        self.ossm = place("ossm", [P, 4, NT], 125.5)
        sig = place("s_sig", [P, 2, 344], 50)
        glu = Project(self, "glu", 4, lambda n, c, half: a["w_glu"].rearrange("(k p) n -> p k n", p=P)[:, :, n * P:(n + 1) * P],
                      ghi, glo, ALL_TILES, [0, 1, 2, 3, 4, 5], blocks=4)
        names = ("rows_in", "dt_in", "b_in", "c_in", "d_in", "u_in", "toep_in", "cleared", "quad", "taken", "v", "act",
                 "kg_added", "ystores", "split_hi", "split_lo", "gated")
        q = {n: self.sem(f"s_{n}") for n in names}
        groups_of = lambda i: slice(i // 2 * 8 + i % 2, i // 2 * 8 + 8, 2)
        quads, kinds = 0, {}
        for kind, n in (("rows", 1), ("U", 8), ("C", 1), ("X", 11), ("kernel", 8), ("G", 8), ("gsum", 16), ("final", 1), ("y", 8),
                        ("ysample", 8), ("turn", 9)):
            kinds[kind] = quads
            quads += n
        with nc.Block() as block:
            @block.sync
            def _(sp):
                for j, src in enumerate(("state_ssm_re", "state_ssm_im")):
                    sp.dma_start(rows[:, j], a[src].rearrange("b g p -> (b g p)").rearrange("(r x) -> r x", x=P)).then_inc(q["rows_in"], 16)
                for j, src in enumerate(("ssm_a_re", "ssm_a_im")):
                    sp.dma_start(rows[0:T, 2 + j], a[src].rearrange("g p -> (g p)").rearrange("(r x) -> r x", x=P)).then_inc(q["rows_in"], 16)
                for e in range(2):
                    sp.dma_start(sm[e * 64:(e + 1) * 64, 0], a["ssm_log_dt"].rearrange("(t e a) -> e a t", e=2, a=1)[e].to_broadcast([64, T]),
                                 allow_slow_non_contiguous=True).then_inc(q["dt_in"], 16)
                sp.wait_ge(q["cleared"], 1)
                sp.dma_start(Us[0:NS, :, 0], self.us_dram.rearrange("b (g c) -> b g c", c=C)).then_inc(q["u_in"], 16)
                sp.dma_start(Us[32:32 + NS, :, L - 1], self.us_dram.rearrange("b (g c) -> b g c", c=C)).then_inc(q["u_in"], 16)
                for j, src in enumerate(("ssm_b_re", "ssm_b_im")):
                    for e in range(2):
                        sp.dma_start(braw[j][e * 64:(e + 1) * 64], a[src].rearrange("(t e) p c -> e p t c", e=2)[e]).then_inc(q["b_in"], 16)
                for j, src in enumerate(("ssm_c_re", "ssm_c_im")):
                    for t_ in range(T):
                        sp.dma_start(crow[j][(t_ % 8) * C:(t_ % 8 + 1) * C, t_ // 8].rearrange("p (e x) -> p e x", e=2),
                                     a[src].rearrange("(t e) c p -> t c e p", e=2)[t_]).then_inc(q["c_in"], 16)
                sp.dma_start(dbc[:, :, :].rearrange("p g c -> p (g c)"),
                             a["ssm_d"].rearrange("(a n) -> a n", a=1).to_broadcast([C, 512])).then_inc(q["d_in"], 16)
                sp.wait_ge(q["kg_added"], 2)
                sp.wait_ge(q["cleared"], 2)
                for l in range(L):
                    sp.dma_start(toep[l * C:(l + 1) * C, :, l * C:P], kg[:, :, 0:(L - l) * C]).then_inc(q["toep_in"], 16)
                sp.wait_ge(q["taken"], kinds["final"] + 1)
                for j, dst in enumerate(("ssm_re_prompt", "ssm_im_prompt")):
                    sp.dma_start(o[dst].rearrange("g p -> (g p)").rearrange("(r x) -> r x", x=P), srows[0:T, j]).then_inc(q["ystores"], 16)
                for j, dst in enumerate(("ssm_re_sample", "ssm_im_sample")):
                    sp.dma_start(o[dst].rearrange("b (t x) -> (b t) x", x=P), srows[:, 2 + j]).then_inc(q["ystores"], 16)
                sp.wait_ge(q["taken"], kinds["turn"])
                glu.sp(sp)
                sp.wait_ge(q["ystores"], 64)

            @block.gpsimd
            def _(pool):
                pool.memset(Us[:, :, :], 0.0).then_inc(q["cleared"], 1)
                pool.wait_ge(q["taken"], kinds["kernel"])
                pool.memset(toep[:, :, :], 0.0).then_inc(q["cleared"], 1)

            @block.scalar
            def _(act):
                glu.credits_drain(act)

                def take(kind, i, out, in_, func=ACT.Copy, last=True, **kw):
                    act.wait_ge(q["quad"], kinds[kind] + i + 1)
                    ins = act.activation(out, in_, func, **kw)
                    if last:
                        ins.then_inc(q["taken"], 1)

                def bank(kind, i):
                    return ps[(kinds[kind] + i) % 4]
                b0 = bank("rows", 0)
                take("rows", 0, s0[:, 0].rearrange("p b t -> p (b t)"), b0[:, 0:P], last=False)
                take("rows", 0, s0[:, 1].rearrange("p b t -> p (b t)"), b0[:, P:2 * P], last=False)
                take("rows", 0, sm[:, 1:3].rearrange("p i t -> p (i t)"), b0[:, 2 * P:2 * P + 2 * T])
                act.wait_ge(q["dt_in"], 32)
                act.activation(sm[:, 0], sm[:, 0], ACT.Exp).then_inc(q["act"], 1)
                act.wait_ge(q["v"], 2)
                act.activation(sm[:, 3], sm[:, 4], ACT.Exp).then_inc(q["act"], 1)
                act.wait_ge(q["v"], self.ssm_angle)
                act.activation(sm[:, 8:10], sm[:, 6:8], ACT.Sin).then_inc(q["act"], 1)
                for i in range(8):
                    take("U", i, U[:, :, i], bank("U", i).rearrange("p (g c) -> p g c", c=C))
                b1 = bank("C", 0)
                take("C", 0, craw[0][:, :, :].rearrange("p t c -> p (t c)"), b1[:, 0:256], last=False)
                take("C", 0, craw[1][:, :, :].rearrange("p t c -> p (t c)"), b1[:, 256:512])
                for i in range(11):
                    n = min(3, G - 3 * i)
                    take("X", i, X[:, 3 * i:3 * i + n].rearrange("p g n -> p (g n)"), bank("X", i)[:, 0:n * XW])
                for i in range(8):
                    take("kernel", i, kg[:, groups_of(i)], bank("kernel", i)[0:C, :].rearrange("p (g n) -> p g n", g=4))
                for i in range(8):
                    take("G", i, gm[i // 4][:, 4 * (i % 4):4 * (i % 4) + 4].rearrange("p t n -> p (t n)"), bank("G", i))
                for i in range(16):
                    b = bank("gsum", i)[:, 0:2 * XW].rearrange("p (i n) -> p i n", i=2)
                    for j in range(2):
                        take("gsum", i, S[j][:, i, 1:SW], b[:, j, 0:P], last=False)
                    take("gsum", i, gsm[:, :, i], b[:, :, XW - NS:XW])
                take("final", 0, srows[0:T, 0:2].rearrange("p i x -> p (i x)"), bank("final", 0)[0:T, 0:2 * P], last=False)
                take("final", 0, srows[:, 2:4].rearrange("p i x -> p (i x)"), bank("final", 0)[:, 2 * P:4 * P])
                for i in range(8):
                    take("y", i, yg[:, :, :].rearrange("p l (g c) -> p g l c", c=C)[:, groups_of(i)],
                         bank("y", i).rearrange("p (g l c) -> p g l c", g=4, l=L), ACT.Gelu_apprx_tanh)
                for i in range(8):
                    take("ysample", i, ys[:, :].rearrange("p (g c) -> p g c", c=C)[:, groups_of(i)],
                         bank("ysample", i)[0:NS].rearrange("p (g n) -> p g n", g=4)[:, :, 0:C], ACT.Gelu_apprx_tanh)
                for i in range(8):
                    take("turn", i, gT[:, :, i:NP:L], bank("turn", i).rearrange("p (k n) -> p k n", k=4))
                take("turn", 8, gT[:, :, NP:NT], bank("turn", 8)[:, 0:4 * NS].rearrange("p (k n) -> p k n", k=4))
                act.wait_ge(q["taken"], kinds["turn"] + 9)
                act.wait_ge(q["ystores"], 64)
                act.activation(ghi[:, :, :], gT[:, :, :], ACT.Copy).then_inc(q["split_hi"], 1)
                glu.act_ahead(act)

                def gate(n, c, tt, t0, size, bank_):
                    m = n * 3 + tt
                    if m >= 2:
                        act.wait_ge(q["gated"], m - 1)
                    act.activation(sig[:, m % 2, 0:size], ps[bank_][:, 0:size], ACT.Sigmoid,
                                   bias=self.b_glu[:, n:n + 1]).then_inc(glu.drained, 1)
                glu.act(act, gate, ahead=False)

            @block.vector
            def _(v):
                glu.credits_dve(v)
                n_v = [0]

                def step(ins):
                    n_v[0] += 1
                    ins.then_inc(q["v"], 1)
                    v.wait_ge(q["v"], n_v[0])

                def tt(out, x, y, op):
                    step(v.tensor_tensor(out, x, y, op))

                def tsc(out, x, s1, s2, op0, op1=None):
                    step(v.tensor_scalar(out, x, s1, s2, op0, op1) if op1 is not None else v.tensor_scalar(out, x, s1, None, op0))

                def cmul(re, im, ar, ai, br, bi, t0, t1, minus_im=False):
                    tt(t0, ar, br, ALU.mult)
                    tt(t1, ai, bi, ALU.mult)
                    tt(re, t0, t1, ALU.subtract)
                    tt(t0, ar, bi, ALU.mult)
                    tt(t1, ai, br, ALU.mult)
                    if minus_im:
                        step(v.scalar_tensor_tensor(out=im, in0=t0, scalar=-1.0, in1=t1, op0=ALU.mult, op1=ALU.subtract))
                    else:
                        tt(im, t0, t1, ALU.add)
                dt, are, lim, mag, lrdt, th, r0, r1, sin, cos = (sm[:, i] for i in range(10))
                w0, w1, w2, den, fre, fim, nr, lre, cre, cim, m8, u_re, u_im = (sm[:, i] for i in range(10, 23))
                v.wait_ge(q["taken"], 1)
                v.wait_ge(q["act"], 1)
                tsc(lre, are, -1e-4, None, ALU.min)
                tt(lrdt, lre, dt, ALU.mult)
                tt(th, lim, dt, ALU.mult)
                tsc(w0, th, 1.0 / (2 * math.pi), None, ALU.mult)
                step(v.tensor_copy(smi[:, :], w0))
                step(v.tensor_copy(w0, smi[:, :]))
                for src_, k_ in ((th, -6.28125), (r0, -PI2_MID), (r0, -PI2_LOW)):
                    step(v.scalar_tensor_tensor(out=r0, in0=w0, scalar=k_, in1=src_, op0=ALU.mult, op1=ALU.add))
                tsc(r1, r0, math.pi / 2, None, ALU.add)
                tsc(w1, r1, math.pi, -2 * math.pi, ALU.is_gt, ALU.mult)
                tt(r1, r1, w1, ALU.add)
                tsc(sm[:, 6:8], sm[:, 6:8], PI_BELOW, -PI_BELOW, ALU.min, ALU.max)
                assert n_v[0] == self.ssm_angle, n_v[0]
                v.wait_ge(q["act"], 3)
                tt(pw[:, 0, 1], mag, cos, ALU.mult)
                tt(pw[:, 1, 1], mag, sin, ALU.mult)
                step(v.memset(pw[:, 0, 0], 1.0))
                step(v.memset(pw[:, 1, 0], 0.0))
                for n in (1, 2, 4):
                    bc = lambda x: x[:, n:n + 1].to_broadcast([P, n, T])
                    sh = lambda x: x[:, 0:n * T].rearrange("p (k t) -> p k t", k=n)
                    cmul(pw[:, 0, n + 1:2 * n + 1], pw[:, 1, n + 1:2 * n + 1], pw[:, 0, 1:n + 1], pw[:, 1, 1:n + 1],
                         bc(pw[:, 0]), bc(pw[:, 1]), sh(tmp[0]), sh(tmp[1]))
                tt(w0, lre, lre, ALU.mult)
                tt(w1, lim, lim, ALU.mult)
                tt(den, w0, w1, ALU.add)
                step(v.reciprocal(den, den))
                tsc(nr, pw[:, 0, 1], -1.0, None, ALU.add)
                tt(w0, nr, lre, ALU.mult)
                tt(w1, pw[:, 1, 1], lim, ALU.mult)
                tt(w0, w0, w1, ALU.add)
                tt(fre, w0, den, ALU.mult)
                tt(w0, pw[:, 1, 1], lre, ALU.mult)
                tt(w1, nr, lim, ALU.mult)
                tt(w0, w0, w1, ALU.subtract)
                tt(fim, w0, den, ALU.mult)
                v.wait_ge(q["b_in"], 64)
                wide = lambda x: x.rearrange("p (t a) -> p t a", a=1).to_broadcast([P, T, C])
                s256 = lambda x: x[:, 0:T * C].rearrange("p (t c) -> p t c", t=T)
                cmul(bb[0][:, :, :], bb[1][:, :, :], wide(fre), wide(fim), braw[0][:, :, :], braw[1][:, :, :], s256(tmp[0]), s256(tmp[1]))
                by_step = lambda x, n: x.rearrange("p k (t a) -> p t k a", a=1).to_broadcast([P, T, n, C])
                by_state = lambda x, n: x[:, :, :].rearrange("p t (a c) -> p t a c", a=1).to_broadcast([P, T, n, C])
                full = lambda x, n: x[:, 0:T * n * C].rearrange("p (t k c) -> p t k c", t=T, k=n)
                v.wait_ge(q["taken"], kinds["C"] + 1)
                cmul(ck[0][:, :, :, :], ck[1][:, :, :, :], by_step(pw[:, 0], L + 1), by_step(pw[:, 1], L + 1),
                     by_state(craw[0], L + 1), by_state(craw[1], L + 1), full(tmp[0], L + 1), full(tmp[1], L + 1), minus_im=True)
                assert n_v[0] == self.ssm_ck, n_v[0]
                cmul(gt[0][:, :, :, :], gt[1][:, :, :, :], by_step(pw[:, 0, L - 1::-1], L), by_step(pw[:, 1, L - 1::-1], L),
                     by_state(bb[0], L), by_state(bb[1], L), full(tmp[0], L), full(tmp[1], L))
                assert n_v[0] == self.ssm_gt, n_v[0]
                v.wait_ge(q["d_in"], 16)
                step(v.tensor_tensor(dbc[:, :, :], dbc[:, :, :],
                                     self.ident[0:C, 0:C].rearrange("p (a c) -> p a c", a=1).to_broadcast([C, G, C]), ALU.mult))
                v.wait_ge(q["taken"], kinds["G"])
                v.tensor_tensor(kg[:, :, 0:C], kg[:, :, 0:C], dbc[:, :, :], ALU.add).then_inc(q["kg_added"], 2)
                def unit(re, im):
                    tt(w0, re, re, ALU.mult)
                    tt(w1, im, im, ALU.mult)
                    tt(w0, w0, w1, ALU.add)
                    tsc(w0, w0, -0.5, 1.5, ALU.mult, ALU.add)
                    tt(re, re, w0, ALU.mult)
                    tt(im, im, w0, ALU.mult)
                cmul(cre, cim, cos, sin, cos, sin, w0, w1)
                cmul(w2, den, cre, cim, cre, cim, w0, w1)
                cmul(u_re, u_im, w2, den, w2, den, w0, w1)
                unit(u_re, u_im)
                tt(m8, mag, mag, ALU.mult)
                tt(m8, m8, m8, ALU.mult)
                tt(m8, m8, m8, ALU.mult)
                v.wait_ge(q["toep_in"], 16 * L)
                step(v.memset(rot[0][:, :, 0:1], 1.0))
                step(v.memset(rot[1][:, :, 0:1], 0.0))
                n, cur, spare = 1, (u_re, u_im), [(cre, cim), (w2, den)]
                while n < P:
                    bcn = lambda x: x.rearrange("p (t a) -> p t a", a=1).to_broadcast([P, T, n])
                    shn = lambda x: x[:, 0:T * n].rearrange("p (t j) -> p t j", t=T)
                    cmul(rot[0][:, :, n:2 * n], rot[1][:, :, n:2 * n], rot[0][:, :, 0:n], rot[1][:, :, 0:n],
                         bcn(cur[0]), bcn(cur[1]), shn(half[0]), shn(half[1]))
                    n *= 2
                    if n < P:
                        nxt, spare = spare[0], spare[::-1]
                        cmul(nxt[0], nxt[1], cur[0], cur[1], cur[0], cur[1], w0, w1)
                        cur = nxt
                        unit(*cur)
                v3 = lambda x: x[:, :].rearrange("p (t j) -> p t j", t=T)
                R0, R1 = rot[0][:, :, :], rot[1][:, :, :]
                g0, g1 = S[0][:, :, 1:SW], S[1][:, :, 1:SW]
                v.wait_ge(q["taken"], kinds["gsum"] + 16)
                tt(v3(t[2]), R0, g0, ALU.mult)
                tt(v3(t[3]), R1, g1, ALU.mult)
                tt(v3(t[0]), v3(t[2]), v3(t[3]), ALU.add)
                tt(v3(t[2]), R0, g1, ALU.mult)
                tt(v3(t[3]), R1, g0, ALU.mult)
                tt(v3(t[1]), v3(t[2]), v3(t[3]), ALU.subtract)
                step(v.tensor_copy(v3(t[2]), m8.rearrange("p (t a) -> p t a", a=1).to_broadcast([P, T, P])))
                step(v.memset(v3(t[2])[:, :, 0:1], 0.0))
                for i in range(2):
                    step(v.tensor_tensor_scan(t[i][:, :], t[2][:, :], t[i][:, :], 0.0, ALU.mult, ALU.add))
                tt(v3(t[2]), R0, v3(t[0]), ALU.mult)
                tt(v3(t[3]), R1, v3(t[1]), ALU.mult)
                tt(g0, v3(t[2]), v3(t[3]), ALU.subtract)
                tt(v3(t[2]), R0, v3(t[1]), ALU.mult)
                tt(v3(t[3]), R1, v3(t[0]), ALU.mult)
                tt(g1, v3(t[2]), v3(t[3]), ALU.add)
                for i in range(2):
                    step(v.memset(S[i][:, :, 0:1], 0.0))
                ar, ai = (pw[:, i, 1:2].to_broadcast([P, NS, T]) for i in range(2))
                cmul(sn[:, 0], sn[:, 1], ar, ai, s0[:, 0], s0[:, 1], sn[:, 2], sn[:, 3])
                for i in range(2):
                    tt(sn[:, i], sn[:, i], gsm[:, i].rearrange("p t b -> p b t"), ALU.add)
                for i in range(2):
                    step(v.tensor_copy(sn[:, 2 + i, 0], S[i][:, :, P:P + 1].rearrange("p t a -> p (t a)")))
                assert n_v[0] == self.ssm_states, n_v[0]
                v.wait_ge(q["split_hi"], 1)
                v.tensor_tensor(glo[:, :, :], gT[:, :, :], ghi[:, :, :].bitcast(F32), ALU.subtract).then_inc(q["split_lo"], 1)
                glu.dve_ahead(v)

                def gated(n, c, tt_, t0, size, bank_):
                    m = n * 3 + tt_
                    v.wait_ge(glu.drained, 6 + m + 1)
                    v.tensor_tensor(self.ossm[:, n, t0:t0 + size], sig[:, m % 2, 0:size], gT[:, n, t0:t0 + size],
                                    ALU.mult).then_inc(q["gated"], 1)
                glu.dve(v, gated, ahead=False)

            @block.tensor
            def _(pe):
                def quad(kind, i):
                    n = kinds[kind] + i
                    if n >= 4:
                        pe.wait_ge(q["taken"], n - 3)
                    return ps[n % 4]

                def done(ins):
                    ins.then_inc(q["quad"], 1)
                mm, turn = pe.matmul, pe.transpose
                pe.wait_ge(q["rows_in"], 64)
                b = quad("rows", 0)
                turn(b[:, 0:P], rows[:, 0], self.ident[:, :])
                turn(b[:, P:2 * P], rows[:, 1], self.ident[:, :])
                turn(b[:, 2 * P:2 * P + T], rows[0:T, 2], self.ident[0:T, 0:T])
                done(turn(b[:, 2 * P + T:2 * P + 2 * T], rows[0:T, 3], self.ident[0:T, 0:T]))
                for l in range(8):
                    b = quad("U", l)
                    for m in range(4):
                        ins = turn(b[:, m * P:(m + 1) * P], self.qkvu[:, 12 + m, l:NP:L], self.ident[:, :])
                    done(ins)
                pe.wait_ge(q["c_in"], 32 * 16)
                b = quad("C", 0)
                for j in range(4):
                    i = turn(b[:, j * P:(j + 1) * P], crow[j // 2][:, j % 2], self.ident[:, :])
                done(i)
                pe.wait_ge(q["taken"], kinds["C"])
                pe.wait_ge(q["u_in"], 32)
                for i in range(11):
                    b = quad("X", i)
                    for m in range(min(3, G - 3 * i)):
                        g = 3 * i + m
                        turn(b[:, m * XW:m * XW + P], U[:, g].rearrange("p l c -> p (l c)"), self.ident[:, :])
                        ins = turn(b[:, m * XW + P:(m + 1) * XW], Us[:, g].rearrange("p l c -> p (l c)"), self.ident[0:40, 0:40])
                    done(ins)
                pe.wait_ge(q["v"], self.ssm_ck)
                for i in range(8):
                    b = quad("kernel", i)
                    for m in range(4):
                        t_, e = i // 2 * 4 + m, i % 2
                        r = slice(e * 64, e * 64 + 64)
                        for j in range(2):
                            ins = mm(b[0:C, m * P:(m + 1) * P], bb[j][r, t_], ck[j][r, t_, 0:L].rearrange("p k c -> p (k c)"), start=j == 0, stop=j == 1)
                    done(ins)
                pe.wait_ge(q["v"], self.ssm_gt)
                for i in range(8):
                    b = quad("G", i)
                    for m in range(4):
                        ins = turn(b[:, m * P:(m + 1) * P], gt[i // 4][:, 4 * (i % 4) + m].rearrange("p l c -> p (l c)"), self.ident[:, :])
                    done(ins)
                pe.wait_ge(q["taken"], kinds["gsum"])
                for t_ in range(T):
                    b = quad("gsum", t_)
                    for j in range(2):
                        for e in range(2):
                            ins = mm(b[e * 64:e * 64 + 64, j * XW:(j + 1) * XW], gm[j][:, t_, e * 64:e * 64 + 64], X[:, 2 * t_ + e], start=True, stop=True)
                    done(ins)
                pe.wait_ge(q["v"], self.ssm_states)
                b = quad("final", 0)
                for i in range(2):
                    turn(b[0:T, i * P:(i + 1) * P], sn[:, 2 + i, 0], self.ident[:, :])
                for i in range(2):
                    ins = turn(b[:, (2 + i) * P:(3 + i) * P], sn[:, i].rearrange("p b t -> p (b t)"), self.ident[:, :])
                done(ins)
                pe.wait_ge(q["toep_in"], 16 * L)
                for kind in ("y", "ysample"):
                    for i in range(8):
                        b = quad(kind, i)
                        for m in range(4):
                            t_, e = i // 2 * 4 + m, i % 2
                            g = 2 * t_ + e
                            r = slice(e * 64, e * 64 + 64)
                            cols = slice(m * P, (m + 1) * P)
                            if kind == "y":
                                out, x, s = b[:, cols], X[:, g, 0:P], [S[j][r, t_, 0:P] for j in range(2)]
                            else:
                                cols = slice(m * P, m * P + C)
                                out, x, s = b[0:NS, cols], X[:, g, P:P + NS], [s0[r, j, :, t_] for j in range(2)]
                            steps = L if kind == "y" else 1
                            mm(out, x, toep[:, g, 0:steps * C], start=True, stop=False)
                            for j in range(2):
                                ins = mm(out, s[j], ck[j][r, t_, 1:steps + 1].rearrange("p k c -> p (k c)"), start=False, stop=j == 1)
                        done(ins)
                pe.wait_ge(q["taken"], kinds["turn"])
                for l in range(8):
                    b = quad("turn", l)
                    for m in range(4):
                        ins = turn(b[:, m * P:(m + 1) * P], yg[:, l, m * P:(m + 1) * P], self.ident[:, :])
                    done(ins)
                b = quad("turn", 8)
                for m in range(4):
                    ins = turn(b[:, m * NS:(m + 1) * NS], ys[:, m * P:(m + 1) * P], self.ident[0:NS, 0:NS])
                done(ins)
                pe.wait_ge(q["taken"], kinds["turn"] + 9)
                pe.wait_ge(q["split_lo"], 1)
                glu.pe(pe)

    def place(self, name, shape, kb, dt=F32, ring=False):
        off = (self.ring_start if ring else self.arena) + int(kb * 1024) // 32 * 32
        size = 4
        for n in shape[1:]:
            size *= n
        assert off + size <= (self.ring_end if ring else self.nc.sbuf_usable_end), name
        return self.nc.alloc_sbuf_tensor_at(name, shape, dt, offset=off)

    def memory(self):
        nc, a, o, ps = self.nc, self.a, self.o, self.ps
        NM = 256
        place = self.place
        rows = place("m_rows", [P, 2, D], 0)
        mT = place("m_T", [P, KD, NM], 8)
        hhi = place("m_hhi", [P, KD, NM], 16, F32R)
        hlo = place("m_hlo", [P, KD, NM], 24, F32R)
        self.mkT = place("mkT", [P, KD, NM], 48)
        mvT = place("m_vT", [P, KD, NM], 32)
        mk = place("m_k", [P, 2, D], 40)
        self.mv = place("mv", [P, 2, D], 56)
        square, tmp, root = (place(f"m_{n}", [P, 2, 256], 81 + 2 * i) for i, n in enumerate(("square", "tmp", "root")))
        aux = place("m_aux", [P, 2, 512], 88)
        norm = Norm(self, "m_n", [(0, NM)], lambda k, t0, n: mT[:, k, t0:t0 + n], KD,
                    lambda k: self.gains[:, 3, k:k + 1], hhi, hlo, square, tmp, root, aux, [4])
        view = lambda n: a[n].rearrange("(k p) n -> p k n", p=P)
        proj = Project(self, "m", 16, lambda n, c, half: view(("w_xk", "w_xv")[c % 2])[:, :, ds(half * P, P)],
                       hhi, hlo, [(0, NM)], [0, 1, 2])
        rows_in, mT_ps, mT_sb, turned, out_sb, stores = (
            self.sem(f"m_{n}") for n in ("rows_in", "T_ps", "T_sb", "turned", "out_sb", "stores"))
        with nc.Block() as block:
            @block.sync
            def _(sp):
                sp.dma_start(rows[:, :, :], a["mem_prompt"].rearrange("(b p) n -> p b n", p=P)).then_inc(rows_in, 16)
                proj.sp(sp)
                for j, (name, src) in enumerate((("mem_k_prompt", mk), ("mem_v_prompt", self.mv))):
                    sp.wait_ge(out_sb, 4 * j + 4)
                    sp.dma_start(o[name].rearrange("(b p) n -> p b n", p=P), src[:, :, :]).then_inc(stores, 16)
                sp.wait_ge(stores, 32)

            @block.scalar
            def _(act):
                proj.credits_drain(act)
                proj.act_ahead(act)
                for i in range(4):
                    act.wait_ge(mT_ps, i + 1)
                    act.activation(mT[:, 2 * i:2 * i + 2].rearrange("p k n -> p (k n)"), ps[4 + i], ACT.Copy).then_inc(mT_sb, 1)
                act.wait_ge(mT_sb, 4)
                norm.act(act)

                def drain(n, c, t, t0, size, bank):
                    dst = (self.mkT, mvT)[c % 2]
                    act.activation(dst[:, ds(proj.half, 1), :], ps[bank][:, 0:size].rearrange("p (a n) -> p a n", a=1),
                                   ACT.Copy).then_inc(proj.drained, 1)
                proj.act(act, drain, ahead=False)
                for i in range(8):
                    act.wait_ge(turned, i + 1)
                    j, b, half = i // 4, i // 2 % 2, i % 2
                    act.activation((mk, self.mv)[j][:, b, half * 512:(half + 1) * 512], ps[4 + i % 4], ACT.Copy).then_inc(out_sb, 1)

            @block.vector
            def _(v):
                proj.credits_dve(v)
                proj.dve_ahead(v)
                norm.dve(v)
                proj.dve(v, ahead=False)

            @block.tensor
            def _(pe):
                pe.wait_ge(rows_in, 16)
                for i in range(4):
                    for m in range(4):
                        k, b = 2 * i + m // 2, m % 2
                        j = pe.transpose(ps[4 + i][:, m * P:(m + 1) * P], rows[:, b, k * P:(k + 1) * P], self.ident[:, :])
                    j.then_inc(mT_ps, 1)
                pe.wait_ge(mT_sb, 4)
                norm.pe(pe)
                norm.ready(pe)
                proj.pe(pe)
                pe.wait_ge(proj.drained, 16 + 3)
                for i in range(8):
                    j, b, half = i // 4, i // 2 % 2, i % 2
                    if i >= 4:
                        pe.wait_ge(out_sb, i - 3)
                    for m in range(4):
                        ins = pe.transpose(ps[4 + i % 4][:, m * P:(m + 1) * P], (self.mkT, mvT)[j][:, half * 4 + m, b * P:(b + 1) * P],
                                           self.ident[:, :])
                    ins.then_inc(turned, 1)

    def add_product(self, name, weight, hi, lo, norm=None, before=None):
        nc, a = self.nc, self.a
        proj = Project(self, name, KD, lambda n, c, half: a[weight].rearrange("(k p) n -> p k n", p=P)[:, :, ds(n * P, P)],
                       hi, lo, ALL_TILES, [0, 1, 2, 3, 4, 5])
        with nc.Block() as block:
            @block.sync
            def _(sp):
                proj.sp(sp)

            @block.scalar
            def _(act):
                proj.act_ahead(act)
                if before:
                    before(act)
                if norm:
                    norm.act(act)
                proj.act(act, ahead=False)

            @block.vector
            def _(v):
                proj.credits_dve(v)
                proj.credits_drain(v)
                proj.dve_ahead(v)
                if norm:
                    norm.dve(v)

                def add(n, c, t, t0, size, bank):
                    x = self.xT[:, ds(n, 1), t0:t0 + size]
                    v.tensor_tensor(x, x, self.ps[bank][:, 0:size].rearrange("p (a n) -> p a n", a=1), ALU.add).then_inc(proj.drained, 1)
                proj.dve(v, add, ahead=False)

            @block.tensor
            def _(pe):
                if norm:
                    norm.pe(pe)
                    norm.ready(pe)
                proj.pe(pe)

    def mix(self):
        place = self.place
        hi = place("mix_hi", [P, KD, NT], 0, F32R)
        lo = place("mix_lo", [P, KD, NT], 81, F32R)
        square = place("mix_square", [P, 2, 344], 113.5)
        tmp = place("mix_tmp", [P, 2, 344], 116.5)
        root = place("mix_root", [P, 3, 344], 119.5)
        aux = place("mix_aux", [P, 2, 512], 33)
        joined = self.sem("mix_joined")
        norm = Norm(self, "mix_n", ALL_TILES * 2, lambda k, t0, n: (self.oT, self.ossm)[k // 4][:, k % 4, t0:t0 + n], 4,
                    lambda k: self.gains[:, 6, k:k + 1], hi, lo, square, tmp, root, aux, [0, 1, 2, 3, 4, 5],
                    first=lambda t: 4 * (t // 3))

        def join(act):
            act.activation(self.oT[:, :, NP:NT], self.osT[:, :, :], ACT.Copy).then_inc(joined, 1)
            act.wait_ge(joined, 1)
        self.add_product("mix", "w_out", hi, lo, norm, join)

    def cross_queries(self):
        nc, a, place = self.nc, self.a, self.place
        self.xhi = place("x_hi", [P, KD, NT], 0, F32R)
        self.xlo = place("x_lo", [P, KD, NT], 64.5, F32R)
        self.qT = place("x_qT", [P, KD, NT], 97)
        square = place("x_square", [P, 2, 344], 129.5)
        tmp = place("x_tmp", [P, 2, 344], 132.5)
        root = place("x_root", [P, 3, 344], 135.5)
        aux = place("x_aux", [P, 2, 512], 33)
        norm = Norm(self, "x_n", ALL_TILES, lambda k, t0, n: self.xT[:, k, t0:t0 + n], KD,
                    lambda k: self.gains[:, 2, k:k + 1], self.xhi, self.xlo, square, tmp, root, aux, [0, 1, 2])
        proj = Project(self, "xq", KD, lambda n, c, half: a["w_xq"].rearrange("(k p) n -> p k n", p=P)[:, :, ds(n * P, P)],
                       self.xhi, self.xlo, ALL_TILES, [0, 1, 2, 3, 4, 5])
        with nc.Block() as block:
            @block.sync
            def _(sp):
                proj.sp(sp)

            @block.scalar
            def _(act):
                proj.credits_drain(act)
                proj.act_ahead(act)
                norm.act(act)

                def drain(n, c, t, t0, size, bank):
                    act.activation(self.qT[:, ds(n, 1), t0:t0 + size],
                                   self.ps[bank][:, 0:size].rearrange("p (a n) -> p a n", a=1), ACT.Copy).then_inc(proj.drained, 1)
                proj.act(act, drain, ahead=False)

            @block.vector
            def _(v):
                proj.credits_dve(v)
                proj.dve_ahead(v)
                norm.dve(v)
                proj.dve(v, ahead=False)

            @block.tensor
            def _(pe):
                norm.pe(pe)
                norm.ready(pe)
                proj.pe(pe)

    def cross(self):
        nc, a, ps, place = self.nc, self.a, self.ps, self.place
        GR, HEADS, NM, SCALE = 8, 4, 256, 1.0 / 16
        p = place("c_p", [P, 2, 4, NM], 32.5)
        pT = place("c_pT", [P, 2, 512], 40.5)
        qrows = place("c_qrows", [NS, D], 40.5)
        masked = place("c_masked", [32, D], 32.5)
        s = place("c_s", [P, 8, NS], 44.5)
        sp_ = place("c_sp", [32, NM], 45)
        pad = place("c_pad", [P, NS, 2, 32], 46)
        mx = place("c_mx", [P, 2, 4], 44.75)
        sums = place("c_sums", [P, 2, 4], 44.8)
        smx = place("c_smx", [32, 2], 44.85)
        sel = place("c_sel", [32, NS], 44.9)
        qb = place("c_qb", [P, 2, D], 129.5)
        mask = place("c_mask", [32, D], 137.5)
        cache = place("c_cache", [P, 4, 2, D], 0, ring=True)
        names = ("q_ps", "q_rows", "q_stored", "sc_ps", "maxed", "exped", "scaled", "turned", "pT", "pv", "o_hi", "o_lo",
                 "product", "reduced", "v_used", "consts", "s_ps", "s_dve", "s_exp", "s_turned", "padded", "all_v", "kept",
                 "columns")
        q = {n: self.sem(f"c_{n}") for n in names}
        cache_in = [self.sem(f"c_cache_in{r}") for r in range(4)]
        qb_in = [self.sem(f"c_qb_in{r}") for r in range(2)]
        with nc.Block() as block:
            @block.sync
            def _(sp):
                def load(n):
                    if n >= 4:
                        if n - 4 < NS:
                            sp.wait_ge(q["reduced"], n - 3)
                        else:
                            sp.wait_ge(q["v_used"], n - 4 - NS + 1)
                    src = a["cache_mem_k" if n < NS else "cache_mem_v"][n % NS].rearrange("(b p) n -> p b n", p=P)
                    sp.dma_start(cache[:, n % 4], src).then_inc(cache_in[n % 4], 16)
                for n in range(4):
                    load(n)
                sp.wait_ge(q["q_rows"], 2)
                sp.dma_start(self.xq_dram, qrows[:, :]).then_inc(q["q_stored"], 16)
                sp.wait_ge(q["q_stored"], 16)
                for n in range(2 * NS):
                    if n < NS:
                        if n >= 2:
                            sp.wait_ge(q["product"], n - 1)
                        sp.dma_start(qb[:, n % 2], self.xq_dram[n:n + 1, :].to_broadcast([P, D])).then_inc(qb_in[n % 2], 16)
                    if n + 4 < 2 * NS:
                        load(n + 4)

            @block.gpsimd
            def _(pool):
                pool.memset(pad[:, :, :, :], 0.0).then_inc(q["consts"], 1)
                pool.memset(mask[:, :], 1.0).then_inc(q["consts"], 1)
                pool.wait_ge(q["consts"], 2)
                m3 = mask[:, :].rearrange("p (h x) -> p h x", h=HEADS)
                pool.affine_select(out=m3, in_=m3, compare_op=ALU.is_ge, fill=0.0, base=0, pattern=[[-8, HEADS], [0, NM]],
                                   channel_multiplier=1).then_inc(q["consts"], 1)
                pool.wait_ge(q["consts"], 3)
                pool.affine_select(out=m3, in_=m3, compare_op=ALU.is_ge, fill=0.0, base=7, pattern=[[8, HEADS], [0, NM]],
                                   channel_multiplier=-1).then_inc(q["consts"], 1)
                for b in range(NS):
                    pool.wait_ge(cache_in[b % 4], 16 * (b // 4 + 1))
                    pool.wait_ge(qb_in[b % 2], 16 * (b // 2 + 1))
                    pool.tensor_tensor(cache[:, b % 4], cache[:, b % 4],
                                       qb[:, b % 2].rearrange("p (a n) -> p a n", a=1).to_broadcast([P, 2, D]),
                                       ALU.mult).then_inc(q["product"], 1)

            @block.scalar
            def _(act):
                for half in range(2):
                    act.wait_ge(q["q_ps"], 1)
                    act.activation(qrows[:, half * 512:(half + 1) * 512], ps[6 + half][0:NS, :], ACT.Copy).then_inc(q["q_rows"], 1)
                for i in range(GR + 2):
                    if i < GR:
                        act.wait_ge(q["maxed"], i + 1)
                        if i >= 2:
                            act.wait_ge(q["turned"], i - 1)
                        for b in range(4):
                            ins = act.activation(p[:, i % 2, b], self.psum[:, (i % 2) * 1024 + b * NM:(i % 2) * 1024 + (b + 1) * NM],
                                                 ACT.Exp, bias=mx[:, i % 2, b:b + 1], scale=SCALE, accum_out=sums[:, i % 2, b:b + 1])
                        ins.then_inc(q["exped"], 1)
                    if 1 <= i <= GR:
                        act.wait_ge(q["turned"], i)
                        act.wait_ge(q["pv"], 2 * (i - 1))
                        if i == 1:
                            act.wait_ge(q["q_stored"], 16)
                        act.activation(pT[:, :, :].rearrange("p b n -> p (b n)"), self.psum[:, 2048:3072], ACT.Copy).then_inc(q["pT"], 1)
                    if i >= 2:
                        h, half = divmod(i - 2, 2)
                        for d in range(2):
                            act.wait_ge(q["pv"], 2 * (i - 2) + d + 1)
                            act.activation(self.xhi[:, 2 * h + d, half * 512:(half + 1) * 512], ps[6 + d], ACT.Copy).then_inc(q["o_hi"], 1)
                act.wait_ge(q["s_dve"], 2)
                act.activation(sp_[:, :], ps[0][0:32, 0:NM], ACT.Exp, bias=smx[:, 0:1], scale=SCALE,
                               accum_out=smx[:, 1:2]).then_inc(q["s_exp"], 1)
                act.wait_ge(q["columns"], 1)
                act.activation(self.xhi[:, :, NP:NT], ps[4][:, 0:KD * NS].rearrange("p (k m) -> p k m", k=KD), ACT.Copy).then_inc(q["o_hi"], 1)

            @block.vector
            def _(v):
                v.tensor_reduce(sel[:, :], self.ident[0:32, 0:32].rearrange("p (h b) -> p b h", b=NS), AX.X, ALU.add).then_inc(q["kept"], 1)
                for i in range(GR + 2):
                    if i < GR:
                        v.wait_ge(q["sc_ps"], i + 1)
                        v.tensor_reduce(mx[:, i % 2], self.psum[:, (i % 2) * 1024:(i % 2 + 1) * 1024].rearrange("p (b n) -> p b n", b=4),
                                        AX.X, ALU.max).then_inc(q["s_ps"], 1)
                        v.wait_ge(q["s_ps"], i + 1)
                        v.tensor_scalar(mx[:, i % 2], mx[:, i % 2], -SCALE, None, ALU.mult).then_inc(q["maxed"], 1)
                        v.wait_ge(q["product"], i + 1)
                        v.tensor_reduce(s[:, :, i], cache[:, i % 4].rearrange("p k (h x) -> p (k h) x", h=HEADS), AX.X,
                                        ALU.add).then_inc(q["reduced"], 1)
                        v.wait_ge(q["exped"], i + 1)
                        v.reciprocal(sums[:, i % 2], sums[:, i % 2]).then_inc(q["padded"], 1)
                        v.wait_ge(q["padded"], i + 1)
                        v.tensor_tensor(p[:, i % 2], p[:, i % 2],
                                        sums[:, i % 2].rearrange("p (b a) -> p b a", a=1).to_broadcast([P, 4, NM]),
                                        ALU.mult).then_inc(q["scaled"], 1)
                    if i >= 2:
                        h, half = divmod(i - 2, 2)
                        for d in range(2):
                            v.wait_ge(q["o_hi"], 2 * (i - 2) + d + 1)
                            v.tensor_tensor(self.xlo[:, 2 * h + d, half * 512:(half + 1) * 512], ps[6 + d],
                                            self.xhi[:, 2 * h + d, half * 512:(half + 1) * 512].bitcast(F32), ALU.subtract).then_inc(q["o_lo"], 1)
                v.wait_ge(q["s_turned"], 1)
                v.tensor_reduce(smx[:, 0:1], ps[0][0:32, 0:NM], AX.X, ALU.max).then_inc(q["s_dve"], 1)
                v.wait_ge(q["s_dve"], 1)
                v.tensor_scalar(smx[:, 0:1], smx[:, 0:1], -SCALE, None, ALU.mult).then_inc(q["s_dve"], 1)
                v.wait_ge(q["s_exp"], 1)
                v.reciprocal(smx[:, 1:2], smx[:, 1:2]).then_inc(q["s_dve"], 1)
                v.wait_ge(q["s_dve"], 3)
                v.tensor_scalar(sp_[:, :], sp_[:, :], smx[:, 1:2], None, ALU.mult).then_inc(q["s_dve"], 1)
                v.wait_ge(q["s_turned"], 2)
                v.wait_ge(q["consts"], 4)
                for b in range(NS):
                    v.tensor_copy(pad[:, b, :, b:32:NS], ps[1][:, 0:64].rearrange("p (k h b) -> p k h b", k=2, b=NS)[:, :, :, b]).then_inc(q["padded"], 1)
                v.wait_ge(q["all_v"], 1)
                v.tensor_tensor(masked[:, :], self.psum[0:32, 1024:2048], mask[:, :], ALU.mult).then_inc(q["kept"], 1)
                v.wait_ge(q["o_hi"], 2 * GR + 1)
                v.tensor_tensor(self.xlo[:, :, NP:NT], ps[4][:, 0:KD * NS].rearrange("p (k m) -> p k m", k=KD),
                                self.xhi[:, :, NP:NT].bitcast(F32), ALU.subtract).then_inc(q["o_lo"], 1)

            @block.tensor
            def _(pe):
                for k in range(KD):
                    ins = pe.transpose(ps[6 + k // 4][0:NS, (k % 4) * P:(k % 4 + 1) * P], self.qT[:, k, NP:NT], self.ident[:, :])
                ins.then_inc(q["q_ps"], 1)
                for i in range(GR + 2):
                    if i < GR:
                        h, half = divmod(i, 2)
                        if i >= 2:
                            pe.wait_ge(q["exped"], i - 1)
                        for b in range(4):
                            for d in range(2):
                                ins = pe.matmul(self.psum[:, (i % 2) * 1024 + b * NM:(i % 2) * 1024 + (b + 1) * NM],
                                                self.qT[:, 2 * h + d, half * 512 + b * P:half * 512 + (b + 1) * P],
                                                self.mkT[:, 2 * h + d], start=d == 0, stop=d == 1)
                        ins.then_inc(q["sc_ps"], 1)
                    if 1 <= i <= GR:
                        pe.wait_ge(q["scaled"], i)
                        pe.wait_ge(q["pT"], i - 1)
                        for b in range(4):
                            for k in range(2):
                                ins = pe.transpose(ps[4 + k][:, b * P:(b + 1) * P], p[:, (i - 1) % 2, b, k * P:(k + 1) * P], self.ident[:, :])
                        ins.then_inc(q["turned"], 1)
                    if i >= 2:
                        h = (i - 2) // 2
                        pe.wait_ge(q["pT"], i - 1)
                        if i == 2:
                            pe.wait_ge(q["q_rows"], 2)
                        for d in range(2):
                            if i > 2:
                                pe.wait_ge(q["o_lo"], 2 * (i - 3) + d + 1)
                            for k in range(2):
                                ins = pe.matmul(ps[6 + d], self.mv[:, k, (2 * h + d) * P:(2 * h + d + 1) * P], pT[:, k],
                                                start=k == 0, stop=k == 1)
                            ins.then_inc(q["pv"], 1)
                pe.wait_ge(q["reduced"], NS)
                for k in range(2):
                    ins = pe.transpose(ps[0][0:32, k * P:(k + 1) * P], s[:, 4 * k:4 * k + 4].rearrange("p h b -> p (h b)"), self.ident[:, :])
                ins.then_inc(q["s_turned"], 1)
                pe.wait_ge(q["s_dve"], 4)
                for k in range(2):
                    ins = pe.transpose(ps[1][:, k * 32:(k + 1) * 32], sp_[:, k * P:(k + 1) * P], self.ident[0:32, 0:32])
                ins.then_inc(q["s_turned"], 1)
                for b in range(NS):
                    pe.wait_ge(q["padded"], GR + b + 1)
                    pe.wait_ge(cache_in[b % 4], 16 * (2 + b // 4 + 1))
                    for k in range(2):
                        for half in range(2):
                            ins = pe.matmul(ps[2 + half][0:32, :], pad[:, b, k], cache[:, b % 4, k, half * 512:(half + 1) * 512],
                                            start=b == 0 and k == 0, stop=b == NS - 1 and k == 1)
                    ins.then_inc(q["all_v"] if b == NS - 1 else q["v_used"], 1)
                pe.wait_ge(q["kept"], 2)
                for k in range(KD):
                    ins = pe.matmul(ps[4][:, k * NS:(k + 1) * NS], masked[:, k * P:(k + 1) * P], sel[:, :], start=True, stop=True)
                ins.then_inc(q["columns"], 1)

    def finish(self):
        nc, o, ps, place = self.nc, self.o, self.ps, self.place
        yT = place("y_T", [P, KD, NT], 0)
        square = place("y_square", [P, 2, 344], 33)
        tmp = place("y_tmp", [P, 2, 344], 36)
        root = place("y_root", [P, 3, 344], 39)
        aux = place("y_aux", [P, 2, 512], 44)
        rows = place("y_rows", [P, 4, D], 50)
        norm = Norm(self, "y_n", ALL_TILES, lambda k, t0, n: self.xT[:, k, t0:t0 + n], KD,
                    lambda k: self.gains[:, 5, k:k + 1], yT, None, square, tmp, root, aux, [0, 1, 2])
        turned, rows_sb = self.sem("y_turned"), self.sem("y_rows_sb")
        stored = [self.sem(f"y_stored{r}") for r in range(4)]
        count = lambda b: P if b < 8 else NS
        with nc.Block() as block:
            @block.sync
            def _(sp):
                for b in range(9):
                    sp.wait_ge(rows_sb, 2 * b + 2)
                    dst = o["y_prompt"][b * P:(b + 1) * P, :] if b < 8 else o["y_sample"]
                    sp.dma_start(dst, rows[0:count(b), b % 4]).then_inc(stored[b % 4], 16)
                for r in range(4):
                    sp.wait_ge(stored[r], 16 * len(range(r, 9, 4)))

            @block.scalar
            def _(act):
                norm.act(act)
                for b in range(9):
                    for half in range(2):
                        act.wait_ge(turned, 2 * b + half + 1)
                        if b >= 4 and half == 0:
                            act.wait_ge(stored[b % 4], 16 * (b // 4))
                        act.activation(rows[0:count(b), b % 4, half * 512:(half + 1) * 512],
                                       ps[4 + (2 * b + half) % 4][0:count(b), :], ACT.Copy).then_inc(rows_sb, 1)

            @block.vector
            def _(v):
                norm.dve(v)

            @block.tensor
            def _(pe):
                norm.pe(pe)
                norm.ready(pe)
                for b in range(9):
                    for half in range(2):
                        n = 2 * b + half
                        if n >= 4:
                            pe.wait_ge(rows_sb, n - 3)
                        for m in range(4):
                            ins = pe.transpose(ps[4 + n % 4][0:count(b), m * P:(m + 1) * P],
                                               yT[:, half * 4 + m, b * P:b * P + count(b)], self.ident[:, :])
                        ins.then_inc(turned, 1)


def build(nc, a, o):
    k = Kernel(nc, a, o)
    with k.ctx:
        for phase in (
                k.samples_ahead,
                lambda: k.ffn("ffn1", PROMPT_TILES, a["w_ffn1_gate"], a["w_ffn1_up"], a["w_ffn1_down"], 0, decode=True),
                k.project_in, k.attention, k.ssm, k.memory, k.mix, k.cross_queries, k.cross,
                lambda: k.add_product("xo", "w_xo", k.xhi, k.xlo),
                lambda: k.ffn("ffn2", ALL_TILES, a["w_ffn2_gate"], a["w_ffn2_up"], a["w_ffn2_down"], 4),
                k.finish):
            with nc.cleanup_on_exit():
                phase()


_INS = ["x_prompt", "x_sample", "cache_k", "cache_v", "state_ssm_re", "state_ssm_im", "cache_mem_k", "cache_mem_v",
        "page_table", "mem_prompt", "g_ffn1", "w_ffn1_gate", "w_ffn1_up", "w_ffn1_down", "g_mix", "w_in", "sb_bias",
        "ssm_a_re", "ssm_a_im", "ssm_log_dt", "ssm_b_re", "ssm_b_im", "ssm_c_re", "ssm_c_im", "ssm_d", "w_glu",
        "b_glu", "g_sb_out", "g_ssm_out", "w_out", "g_xattn", "g_mem", "w_xq", "w_xk", "w_xv", "w_xo", "g_ffn2",
        "w_ffn2_gate", "w_ffn2_up", "w_ffn2_down", "g_final"]
_OUTS = [("y_prompt", (1024, 1024), (1, 1024, 1024)), ("y_sample", (8, 1024), (8, 1, 1024)),
         ("k_prompt", (1024, 512), (1, 1, 1024, 8, 64)), ("v_prompt", (1024, 512), (1, 1, 1024, 8, 64)),
         ("k_sample", (8, 512), (1, 8, 1, 8, 64)), ("v_sample", (8, 512), (1, 8, 1, 8, 64)),
         ("ssm_re_prompt", (32, 64), (1, 1, 32, 64)), ("ssm_im_prompt", (32, 64), (1, 1, 32, 64)),
         ("ssm_re_sample", (8, 2048), (1, 8, 32, 64)), ("ssm_im_sample", (8, 2048), (1, 8, 32, 64)),
         ("mem_k_prompt", (256, 1024), (1, 1, 256, 4, 256)), ("mem_v_prompt", (256, 1024), (1, 1, 256, 4, 256))]
_SHAPES = {"x_prompt": (1024, 1024), "x_sample": (8, 1024), "cache_k": (640, 128, 512), "cache_v": (640, 128, 512),
           "mem_prompt": (256, 1024), "cache_mem_k": (8, 256, 1024), "cache_mem_v": (8, 256, 1024)}


def _shape(name, a):
    if name in _SHAPES:
        return _SHAPES[name]
    return a.shape[1:] if a.ndim > 1 and a.shape[0] == 1 else a.shape


def kernel(**inputs):
    import numpy as _np
    import concourse.bacc as _bacc
    from concourse import mybir as _mybir
    from concourse.bass_utils import run_bass_kernel_spmd as _run

    nc = _bacc.Bacc("TRN2", target_bir_lowering=False, num_devices=1)
    arrays, a, o = {}, {}, {}
    for name in _INS:
        x = _np.ascontiguousarray(inputs[name]).reshape(_shape(name, _np.asarray(inputs[name])))
        arrays[f"in_{name}_dram"] = x
        a[name] = nc.dram_tensor(f"in_{name}_dram", x.shape, _mybir.dt.from_np(x.dtype), kind="ExternalInput").ap()
    for name, shape, _ in _OUTS:
        o[name] = nc.dram_tensor(f"out_{name}_dram", shape, F32, kind="ExternalOutput").ap()
    build(nc, a, o)
    r = _run(nc, [arrays], core_ids=[0])
    return tuple(r.results[0][f"out_{name}_dram"].reshape(full) for name, _, full in _OUTS)
```
